# Optimizing a Trainium2 kernel written in Bass

```python
import jax, jax.numpy as jnp
from jax import lax
import numpy as np
import math
import jax
import jax.numpy as jnp

D_MODEL = 1024
BATCH = 1
SEQ = 256
DEPTH = 4

N_MIXERS = 3
EXPAND = 2
D_INNER = EXPAND * D_MODEL
CONF_KERNEL = 31
SHORT_KERNEL = 3
FOX_HEADS = 16
FOX_HEAD_DIM = D_INNER // FOX_HEADS
Q_BLOCK = 128
NORM_EPS = 1e-6
N_A = (DEPTH + 2) // 3
N_B = (DEPTH + 1) // 3
N_C = DEPTH // 3


def rms_norm(x, g):
    xf = x.astype(jnp.float32)
    y = xf * lax.rsqrt(jnp.mean(xf * xf, axis=-1, keepdims=True) + NORM_EPS)
    return (y * g.astype(jnp.float32)).astype(x.dtype)

def layer_norm(x, g, b):
    xf = x.astype(jnp.float32)
    mu = jnp.mean(xf, axis=-1, keepdims=True)
    var = jnp.mean(jnp.square(xf - mu), axis=-1, keepdims=True)
    y = (xf - mu) * lax.rsqrt(var + NORM_EPS)
    return (y * g.astype(jnp.float32) + b.astype(jnp.float32)).astype(x.dtype)

def causal_depthwise_conv(x, w):
    k_width, channels = w.shape
    kern = w[:, None, :].astype(x.dtype)
    return lax.conv_general_dilated(
        x, kern, window_strides=(1,), padding=[(k_width - 1, 0)],
        dimension_numbers=("NWC", "WIO", "NWC"), feature_group_count=channels)

def conformer_conv_mixer(h, w_in, conv_w, conv_b, ln_g, ln_b, w_out):
    proj = h @ w_in
    val, glu_gate, z = jnp.split(proj, 3, axis=-1)
    u = val * jax.nn.sigmoid(glu_gate)
    u = causal_depthwise_conv(u, conv_w) + conv_b
    u = jax.nn.silu(layer_norm(u, ln_g, ln_b))
    return (u * jax.nn.silu(z)) @ w_out

def blocked_forgetting_attention(q, k, v, c):
    b, s_len, n_h, d_h = q.shape
    n_blocks = s_len // Q_BLOCK
    scale = d_h ** -0.5
    k_pos = jnp.arange(s_len)

    def one_block(i):
        start = i * Q_BLOCK
        q_blk = lax.dynamic_slice_in_dim(q, start, Q_BLOCK, axis=1)
        c_blk = lax.dynamic_slice_in_dim(c, start, Q_BLOCK, axis=2)
        logits = jnp.einsum("bqhd,bkhd->bhqk", q_blk, k,
                            preferred_element_type=jnp.float32) * scale
        logits = logits + c_blk[..., :, None] - c[..., None, :]
        q_pos = start + jnp.arange(Q_BLOCK)
        causal = k_pos[None, :] <= q_pos[:, None]
        logits = jnp.where(causal, logits, -jnp.inf)
        p = jax.nn.softmax(logits, axis=-1)
        return jnp.einsum("bhqk,bkhd->bqhd", p.astype(v.dtype), v)

    out = lax.map(one_block, jnp.arange(n_blocks))
    return out.transpose(1, 0, 2, 3, 4).reshape(b, s_len, n_h, d_h)

def forgetting_attention_mixer(h, w_in, f_bias, q_norm_g, k_norm_g, w_out):
    b, s_len, _ = h.shape
    proj = h @ w_in
    q, k, v, z, f_logit = jnp.split(
        proj, [D_INNER, 2 * D_INNER, 3 * D_INNER, 4 * D_INNER], axis=-1)
    q = rms_norm(q.reshape(b, s_len, FOX_HEADS, FOX_HEAD_DIM), q_norm_g)
    k = rms_norm(k.reshape(b, s_len, FOX_HEADS, FOX_HEAD_DIM), k_norm_g)
    v = v.reshape(b, s_len, FOX_HEADS, FOX_HEAD_DIM)
    log_f = jax.nn.log_sigmoid((f_logit + f_bias).astype(jnp.float32))
    c = jnp.cumsum(log_f, axis=1).transpose(0, 2, 1)
    o = blocked_forgetting_attention(q, k, v, c).reshape(b, s_len, D_INNER)
    return (o * jax.nn.silu(z)) @ w_out

def short_conv_mixer(h, w_in, conv_w, w_out):
    proj = h @ w_in
    u, b_gate, c_gate, z = jnp.split(proj, 4, axis=-1)
    y = b_gate * causal_depthwise_conv(c_gate * u, conv_w)
    return (y * jax.nn.silu(z)) @ w_out

def first_inputs(seed: int = 0) -> dict:
    key = jax.random.key(seed)
    ks = jax.random.split(key, 20)
    f32 = jnp.float32
    nrm = lambda k, shape, s: jax.random.normal(k, shape, f32) * s
    d, e, h = D_MODEL, D_INNER, FOX_HEADS
    return {
        "x": jax.random.normal(ks[0], (BATCH, SEQ, d), f32),
        "a_norm": 1.0 + nrm(ks[1], (N_A, d), 0.05),
        "a_w_in": nrm(ks[2], (N_A, d, 3 * e), d ** -0.5),
        "a_conv_w": nrm(ks[3], (N_A, CONF_KERNEL, e), CONF_KERNEL ** -0.5),
        "a_conv_b": nrm(ks[4], (N_A, e), 0.01),
        "a_ln_g": 1.0 + nrm(ks[5], (N_A, e), 0.05),
        "a_ln_b": nrm(ks[6], (N_A, e), 0.01),
        "a_w_out": nrm(ks[7], (N_A, e, d), e ** -0.5),
        "b_norm": 1.0 + nrm(ks[8], (N_B, d), 0.05),
        "b_w_in": nrm(ks[9], (N_B, d, 4 * e + h), d ** -0.5),
        "b_f_bias": 2.0 + nrm(ks[10], (N_B, h), 0.5),
        "b_q_norm": 1.0 + nrm(ks[11], (N_B, FOX_HEAD_DIM), 0.05),
        "b_k_norm": 1.0 + nrm(ks[12], (N_B, FOX_HEAD_DIM), 0.05),
        "b_w_out": nrm(ks[13], (N_B, e, d), e ** -0.5),
        "c_norm": 1.0 + nrm(ks[14], (N_C, d), 0.05),
        "c_w_in": nrm(ks[15], (N_C, d, 4 * e), d ** -0.5),
        "c_conv_w": nrm(ks[16], (N_C, SHORT_KERNEL, e), SHORT_KERNEL ** -0.5),
        "c_w_out": nrm(ks[17], (N_C, e, d), e ** -0.5),
    }

def first_block(x, a_norm, a_w_in, a_conv_w, a_conv_b, a_ln_g, a_ln_b, a_w_out,
              b_norm, b_w_in, b_f_bias, b_q_norm, b_k_norm, b_w_out,
              c_norm, c_w_in, c_conv_w, c_w_out):
    for i in range(DEPTH):
        kind, j = i % N_MIXERS, i // N_MIXERS
        if kind == 0:
            hn = rms_norm(x, a_norm[j])
            x = x + conformer_conv_mixer(hn, a_w_in[j], a_conv_w[j], a_conv_b[j],
                                         a_ln_g[j], a_ln_b[j], a_w_out[j])
        elif kind == 1:
            hn = rms_norm(x, b_norm[j])
            x = x + forgetting_attention_mixer(hn, b_w_in[j], b_f_bias[j], b_q_norm[j],
                                               b_k_norm[j], b_w_out[j])
        else:
            hn = rms_norm(x, c_norm[j])
            x = x + short_conv_mixer(hn, c_w_in[j], c_conv_w[j], c_w_out[j])
    return x


DEPTH_2 = 2

A_HEADS = 8
A_HEAD_DIM = 64
IDX_HEADS = 8
IDX_DIM = 64
TOPK_MAX = 256
B_HEADS = 8
Q_RANK = 256
KV_RANK = 128
NOPE_DIM = 64
ROPE_DIM = 32
V_DIM = 64
ROPE_THETA = 10000.0
NUM_BUCKETS = 32
MAX_DISTANCE = 128
D_FF = 2816
CONV_WIDTH = 3
LN_EPS = 1e-5
RMS_EPS = 1e-6
DEEPNORM_ALPHA = (2 * DEPTH_2) ** 0.25
DEEPNORM_BETA = (8 * DEPTH_2) ** -0.25
A_WIDTH = A_HEADS * A_HEAD_DIM
B_WIDTH = B_HEADS * V_DIM
SPLIT_SIZES = (A_WIDTH, A_WIDTH, A_WIDTH, IDX_HEADS * IDX_DIM, IDX_DIM, IDX_HEADS,
               Q_RANK, KV_RANK, ROPE_DIM, D_MODEL, D_MODEL)
IN_WIDTH = sum(SPLIT_SIZES)


def layer_norm_2(x, g, b):
    xf = x.astype(jnp.float32)
    mu = jnp.mean(xf, axis=-1, keepdims=True)
    var = jnp.mean(jnp.square(xf - mu), axis=-1, keepdims=True)
    return ((xf - mu) * lax.rsqrt(var + LN_EPS)).astype(x.dtype) * g + b

def rms_norm_2(x, g):
    xf = x.astype(jnp.float32)
    return (xf * lax.rsqrt(jnp.mean(xf * xf, axis=-1, keepdims=True) + RMS_EPS)).astype(x.dtype) * g

def apply_rope(x, positions):
    half = ROPE_DIM // 2
    inv_freq = ROPE_THETA ** (-jnp.arange(half, dtype=jnp.float32) * (2.0 / ROPE_DIM))
    ang = positions.astype(jnp.float32)[:, :, None] * inv_freq
    ang = ang.reshape(ang.shape[:2] + (1,) * (x.ndim - 3) + (half,))
    cos, sin = jnp.cos(ang), jnp.sin(ang)
    x1 = x[..., :half].astype(jnp.float32)
    x2 = x[..., half:].astype(jnp.float32)
    return jnp.concatenate([x1 * cos - x2 * sin, x1 * sin + x2 * cos], axis=-1).astype(x.dtype)

def t5_bucket(rel):
    n = jnp.maximum(rel, 0)
    max_exact = NUM_BUCKETS // 2
    log_ratio = jnp.log(jnp.maximum(n, 1).astype(jnp.float32) / max_exact) / math.log(MAX_DISTANCE / max_exact)
    large = max_exact + (log_ratio * (NUM_BUCKETS - max_exact)).astype(jnp.int32)
    large = jnp.minimum(large, NUM_BUCKETS - 1)
    return jnp.where(n < max_exact, n, large)

def dsa_attention(qa, ka, va, iq, ik, iw, positions, rel_bias):
    bsz, seq = qa.shape[0], qa.shape[1]
    topk = min(TOPK_MAX, seq // 4)
    n_blocks = seq // Q_BLOCK
    key_idx = jnp.arange(seq, dtype=jnp.int32)
    a_scale = A_HEAD_DIM ** -0.5
    i_scale = IDX_DIM ** -0.5
    gather = jax.vmap(lambda t, ii: t[ii])

    def block(i):
        start = i * Q_BLOCK
        q = lax.dynamic_slice_in_dim(qa, start, Q_BLOCK, axis=1)
        q_i = lax.dynamic_slice_in_dim(iq, start, Q_BLOCK, axis=1)
        w_i = lax.dynamic_slice_in_dim(iw, start, Q_BLOCK, axis=1)
        q_pos = lax.dynamic_slice_in_dim(positions, start, Q_BLOCK, axis=1)
        q_idx = start + jnp.arange(Q_BLOCK, dtype=jnp.int32)
        causal = key_idx[None, :] <= q_idx[:, None]
        head_scores = jax.nn.relu(jnp.einsum('bqhd,bsd->bqhs', q_i, ik) * i_scale)
        scores = jnp.einsum('bqhs,bqh->bqs', head_scores, w_i).astype(jnp.float32)
        scores = jnp.where(causal[None], scores, -jnp.inf)
        _, sel = lax.top_k(scores, topk)
        valid = sel <= q_idx[None, :, None]
        k_sel = gather(ka, sel)
        v_sel = gather(va, sel)
        k_pos = gather(positions, sel)
        bias = rel_bias[t5_bucket(q_pos[:, :, None] - k_pos)]
        logits = (jnp.einsum('bqhd,bqkhd->bqkh', q, k_sel).astype(jnp.float32) * a_scale
                  + bias.astype(jnp.float32))
        logits = jnp.where(valid[..., None], logits, -jnp.inf)
        p = jax.nn.softmax(logits, axis=2).astype(va.dtype)
        return jnp.einsum('bqkh,bqkhd->bqhd', p, v_sel)

    out = lax.map(block, jnp.arange(n_blocks, dtype=jnp.int32))
    return out.transpose(1, 0, 2, 3, 4).reshape(bsz, seq, A_WIDTH)

def mla_attention(q_nope, q_rope, k_nope, k_rope, v):
    bsz, seq = q_nope.shape[0], q_nope.shape[1]
    n_blocks = seq // Q_BLOCK
    key_idx = jnp.arange(seq, dtype=jnp.int32)
    scale = (NOPE_DIM + ROPE_DIM) ** -0.5

    def block(i):
        start = i * Q_BLOCK
        qn = lax.dynamic_slice_in_dim(q_nope, start, Q_BLOCK, axis=1)
        qr = lax.dynamic_slice_in_dim(q_rope, start, Q_BLOCK, axis=1)
        q_idx = start + jnp.arange(Q_BLOCK, dtype=jnp.int32)
        causal = key_idx[None, :] <= q_idx[:, None]
        logits = (jnp.einsum('bqhd,bshd->bhqs', qn, k_nope)
                  + jnp.einsum('bqhr,bsr->bhqs', qr, k_rope)).astype(jnp.float32) * scale
        logits = jnp.where(causal[None, None], logits, -jnp.inf)
        p = jax.nn.softmax(logits, axis=-1).astype(v.dtype)
        return jnp.einsum('bhqs,bshd->bqhd', p, v)

    out = lax.map(block, jnp.arange(n_blocks, dtype=jnp.int32))
    return out.transpose(1, 0, 2, 3, 4).reshape(bsz, seq, B_WIDTH)

def token_mixer(h, positions, rel_bias, w_in, q_norm_g, w_uq, kv_norm_g, w_ukv,
                w_branch_a, w_branch_b, w_out):
    bsz, seq = h.shape[0], h.shape[1]
    proj = h @ w_in
    split_at = np.cumsum(SPLIT_SIZES)[:-1].tolist()
    qa, ka, va, iq, ik, iw, cq, ckv, kr, ga, gb = jnp.split(proj, split_at, axis=-1)
    heads_a = (bsz, seq, A_HEADS, A_HEAD_DIM)
    ya = dsa_attention(qa.reshape(heads_a), ka.reshape(heads_a), va.reshape(heads_a),
                       iq.reshape(bsz, seq, IDX_HEADS, IDX_DIM), ik,
                       iw * (IDX_HEADS ** -0.5), positions, rel_bias)
    q = (rms_norm_2(cq, q_norm_g) @ w_uq).reshape(bsz, seq, B_HEADS, NOPE_DIM + ROPE_DIM)
    q_nope, q_rope = q[..., :NOPE_DIM], apply_rope(q[..., NOPE_DIM:], positions)
    kv = (rms_norm_2(ckv, kv_norm_g) @ w_ukv).reshape(bsz, seq, B_HEADS, NOPE_DIM + V_DIM)
    k_nope, v = kv[..., :NOPE_DIM], kv[..., NOPE_DIM:]
    k_rope = apply_rope(kr, positions)
    yb = mla_attention(q_nope, q_rope, k_nope, k_rope, v)
    merged = jax.nn.sigmoid(ga) * (ya @ w_branch_a) + jax.nn.sigmoid(gb) * (yb @ w_branch_b)
    return merged @ w_out

def conv_ffn(h, w_up, conv_w, conv_b, w_down):
    u = h @ w_up
    ch = u.shape[-1]
    u = lax.conv_general_dilated(u, conv_w[:, None, :], window_strides=(1,),
                                 padding=[(CONV_WIDTH - 1, 0)],
                                 dimension_numbers=('NWC', 'WIO', 'NWC'),
                                 feature_group_count=ch) + conv_b
    g, val = jnp.split(u, 2, axis=-1)
    return (jax.nn.silu(g) * val) @ w_down

def second_inputs(seed: int = 0) -> dict:
    key = jax.random.key(seed)
    ks = jax.random.split(key, 24)
    f32 = jnp.float32

    def nrm(k, shape, scale):
        return jax.random.normal(k, shape, f32) * scale

    x = nrm(ks[0], (BATCH, SEQ, D_MODEL), 1.0)
    c = nrm(ks[1], (BATCH, D_MODEL), 1.0)
    offset = jax.random.randint(ks[2], (BATCH, 1), 0, 1024, dtype=jnp.int32)
    positions = offset + jnp.arange(SEQ, dtype=jnp.int32)[None, :]
    rel_bias = nrm(ks[3], (NUM_BUCKETS, A_HEADS), 0.2)
    w_ada = nrm(ks[4], (DEPTH_2, D_MODEL, 6 * D_MODEL), 0.5 * D_MODEL ** -0.5)
    b_ada = nrm(ks[5], (DEPTH_2, 6 * D_MODEL), 0.01)
    w_in = nrm(ks[6], (DEPTH_2, D_MODEL, IN_WIDTH), D_MODEL ** -0.5)
    q_norm_g = 1.0 + nrm(ks[7], (DEPTH_2, Q_RANK), 0.01)
    w_uq = nrm(ks[8], (DEPTH_2, Q_RANK, B_HEADS * (NOPE_DIM + ROPE_DIM)), Q_RANK ** -0.5)
    kv_norm_g = 1.0 + nrm(ks[9], (DEPTH_2, KV_RANK), 0.01)
    w_ukv = nrm(ks[10], (DEPTH_2, KV_RANK, B_HEADS * (NOPE_DIM + V_DIM)), KV_RANK ** -0.5)
    w_branch_a = nrm(ks[11], (DEPTH_2, A_WIDTH, D_MODEL), A_WIDTH ** -0.5)
    w_branch_b = nrm(ks[12], (DEPTH_2, B_WIDTH, D_MODEL), B_WIDTH ** -0.5)
    w_out = nrm(ks[13], (DEPTH_2, D_MODEL, D_MODEL), DEEPNORM_BETA * D_MODEL ** -0.5)
    ln1_g = 1.0 + nrm(ks[14], (DEPTH_2, D_MODEL), 0.01)
    ln1_b = nrm(ks[15], (DEPTH_2, D_MODEL), 0.01)
    w_up = nrm(ks[16], (DEPTH_2, D_MODEL, 2 * D_FF), D_MODEL ** -0.5)
    conv_w = nrm(ks[17], (DEPTH_2, CONV_WIDTH, 2 * D_FF), CONV_WIDTH ** -0.5)
    conv_b = nrm(ks[18], (DEPTH_2, 2 * D_FF), 0.01)
    w_down = nrm(ks[19], (DEPTH_2, D_FF, D_MODEL), DEEPNORM_BETA * D_FF ** -0.5)
    ln2_g = 1.0 + nrm(ks[20], (DEPTH_2, D_MODEL), 0.01)
    ln2_b = nrm(ks[21], (DEPTH_2, D_MODEL), 0.01)
    return {"x": x, "c": c, "positions": positions, "rel_bias": rel_bias,
            "w_ada": w_ada, "b_ada": b_ada, "w_in": w_in,
            "q_norm_g": q_norm_g, "w_uq": w_uq, "kv_norm_g": kv_norm_g, "w_ukv": w_ukv,
            "w_branch_a": w_branch_a, "w_branch_b": w_branch_b, "w_out": w_out,
            "ln1_g": ln1_g, "ln1_b": ln1_b,
            "w_up": w_up, "conv_w": conv_w, "conv_b": conv_b, "w_down": w_down,
            "ln2_g": ln2_g, "ln2_b": ln2_b}

def second_block(x, c, positions, rel_bias, w_ada, b_ada, w_in, q_norm_g, w_uq, kv_norm_g, w_ukv,
              w_branch_a, w_branch_b, w_out, ln1_g, ln1_b, w_up, conv_w, conv_b, w_down,
              ln2_g, ln2_b):
    for l in range(DEPTH_2):
        mod = jax.nn.silu(c) @ w_ada[l] + b_ada[l]
        sh1, sc1, g1, sh2, sc2, g2 = jnp.split(mod[:, None, :], 6, axis=-1)
        h = x * (1.0 + sc1) + sh1
        y = token_mixer(h, positions, rel_bias, w_in[l], q_norm_g[l], w_uq[l], kv_norm_g[l], w_ukv[l],
                        w_branch_a[l], w_branch_b[l], w_out[l])
        x = layer_norm_2(DEEPNORM_ALPHA * x + g1 * y, ln1_g[l], ln1_b[l])
        h = x * (1.0 + sc2) + sh2
        y = conv_ffn(h, w_up[l], conv_w[l], conv_b[l], w_down[l])
        x = layer_norm_2(DEEPNORM_ALPHA * x + g2 * y, ln2_g[l], ln2_b[l])
    return x


def setup_inputs(seed=0):
    out = dict(first_inputs(seed))
    for name, value in second_inputs(seed + 1).items():
        if name != "x":
            out[name + "_2"] = value
    return out


def reference(
    x, a_norm, a_w_in, a_conv_w, a_conv_b, a_ln_g, a_ln_b, a_w_out, b_norm, b_w_in, b_f_bias,
    b_q_norm, b_k_norm, b_w_out, c_norm, c_w_in, c_conv_w, c_w_out, c_2, positions_2,
    rel_bias_2, w_ada_2, b_ada_2, w_in_2, q_norm_g_2, w_uq_2, kv_norm_g_2, w_ukv_2,
    w_branch_a_2, w_branch_b_2, w_out_2, ln1_g_2, ln1_b_2, w_up_2, conv_w_2, conv_b_2, w_down_2,
    ln2_g_2, ln2_b_2,
):
    x = first_block(
        x, a_norm, a_w_in, a_conv_w, a_conv_b, a_ln_g, a_ln_b, a_w_out, b_norm, b_w_in,
        b_f_bias, b_q_norm, b_k_norm, b_w_out, c_norm, c_w_in, c_conv_w, c_w_out,
    )
    return second_block(
        x, c_2, positions_2, rel_bias_2, w_ada_2, b_ada_2, w_in_2, q_norm_g_2, w_uq_2,
        kv_norm_g_2, w_ukv_2, w_branch_a_2, w_branch_b_2, w_out_2, ln1_g_2, ln1_b_2, w_up_2,
        conv_w_2, conv_b_2, w_down_2, ln2_g_2, ln2_b_2,
    )


_drawn_inputs = setup_inputs


def setup_inputs(seed=0):
    import zlib

    import numpy as np

    out = dict(_drawn_inputs(seed))
    spreads = {}
    factors = {'a_conv_b': 4.407,
     'a_ln_b': 8.0,
     'b_q_norm': 4.319,
     'b_k_norm': 4.913,
     'rel_bias_2': 8.0,
     'b_ada_2': 8.0,
     'q_norm_g_2': 8.0,
     'w_uq_2': 4.513,
     'kv_norm_g_2': 8.0,
     'ln1_g_2': 3.886,
     'ln1_b_2': 4.175,
     'conv_b_2': 8.0,
     'ln2_g_2': 3.791,
     'ln2_b_2': 4.058}
    for name, (base, spread) in spreads.items():
        noise = np.random.default_rng([zlib.crc32(name.encode()), seed]).standard_normal(out[name].shape)
        drawn = base * np.exp(spread * noise) if base else spread * noise
        out[name] = jnp.asarray(drawn.astype(out[name].dtype))
    for name, factor in factors.items():
        out[name] = (out[name] * factor).astype(out[name].dtype)
    return out
```

```python
import math
from contextlib import ExitStack

import numpy as np

import concourse.bass as bass
from concourse import mybir

F32 = mybir.dt.float32
F32R = mybir.dt.float32r
I32 = mybir.dt.int32
ALU = mybir.AluOpType
ACT = mybir.ActivationFunctionType
AX = mybir.AxisListType.X

T = 256
D = 1024
E = 2048
NEG = -1.0e30
PICKED = -3.4e38
ALPHA = 4.0 ** 0.25
PIECE = 1024
NRAW = 6
NHL = 6
LOOK = 4
MAGIC = 12582912.0
TWO_PI = [6.28125, 0.0019350051879882812, 3.019916050561733e-07]

CONSTS = (
    [(f"a_norm{j}", 8) for j in range(2)]
    + [(f"a_conv_w{j}", 31 * 16) for j in range(2)]
    + [(f"{n}{j}", 16) for n in ("a_conv_b", "a_ln_g", "a_ln_b") for j in range(2)]
    + [("b_norm", 8), ("b_q_norm", 1), ("b_k_norm", 1), ("b_f_bias", 1), ("c_norm", 8), ("c_conv_w", 48)]
    + [(f"b_ada{l}", 48) for l in range(2)]
    + [(f"conv_w{l}", 132) for l in range(2)]
    + [(f"conv_b{l}", 44) for l in range(2)]
    + [(f"{n}{l}", 8) for n in ("ln1_g", "ln1_b", "ln2_g", "ln2_b") for l in range(2)]
    + [(f"q_norm{l}", 2) for l in range(2)]
    + [(f"kv_norm{l}", 1) for l in range(2)]
    + [("c", 8), ("rel_bias", 256), ("ident", 128), ("cmask", 384), ("onehot", 31), ("ones", 128), ("freq", 1),
       ("ropemul", 2)]
)
COFF = {}
_at = 0
for _name, _n in CONSTS:
    COFF[_name] = (_at, _n)
    _at += _n
NCONST = _at


def bucket_starts():
    n = np.arange(0, 129).astype(np.float32)
    ratio = np.log(np.maximum(n, 1) / np.float32(16)) / np.float32(math.log(128 / 16))
    large = np.minimum(16 + (ratio * np.float32(16)).astype(np.int32), 31)
    large = np.where(n < 16, 0, large)
    return [int(np.argmax(large >= b)) for b in range(16, 32)]


class Eng:

    def __init__(self, sem):
        self.sem, self.n, self.q, self.seen = sem, 0, [], {}

    def wait(self, *toks):
        for t in toks:
            if t is None:
                continue
            if isinstance(t, list):
                self.wait(*t)
                continue
            sem, val = t
            if self.seen.get(sem.name, 0) < val:
                self.seen[sem.name] = val
                self.q.append((0, sem, val))

    def do(self, f, *toks):
        self.wait(*toks)
        self.n += 1
        self.q.append((1, f, self.sem, 1))
        return (self.sem, self.n)

    def quiet(self, f, *toks):
        self.wait(*toks)
        self.q.append((1, f, None, 0))

    def dma(self, f, sem, count, *toks):
        self.wait(*toks)
        self.q.append((1, f, sem, 16))
        return (sem, count)

    def play(self, e):
        for item in self.q:
            if item[0] == 0:
                e.wait_ge(item[1], item[2])
            else:
                ins = item[1](e)
                if item[2] is not None:
                    ins.then_inc(item[2], item[3])


class Buf:

    def __init__(self, ap):
        self.ap, self.free, self.held = ap, [], False

    def release(self, toks):
        self.free, self.held = toks, False


class Ring:

    def __init__(self, aps):
        self.b, self.i = [Buf(a) for a in aps], 0

    def take(self):
        for _ in self.b:
            b = self.b[self.i % len(self.b)]
            self.i += 1
            if not b.held:
                b.held = True
                return b
        raise RuntimeError("every buffer of the ring is held")


def build(nc, w_stream_of, cst, posr, xin, out, dbg=None):
    with ExitStack() as ctx:
        def sb(name, shape, dt=F32):
            return ctx.enter_context(nc.sbuf_tensor(name, shape, dt))

        mem = dict(
            C=sb("C", [128, NCONST]),
            X=sb("X", [128, 8, T]),
            XS=sb("XS", [128, 8, 2 * T], F32R),
            B=[sb(f"B{i}", [128, 4096]) for i in range(4)],
            raw=[sb(f"raw{i}", [128, PIECE]) for i in range(NRAW)],
            wh=[sb(f"wh{i}", [128, PIECE], F32R) for i in range(NHL)],
            wl=[sb(f"wl{i}", [128, PIECE], F32R) for i in range(NHL)],
            os=[sb(f"os{i}", [128, 2 * T], F32R) for i in range(3)],
            t=[sb(f"tmp{i}", [128, 512]) for i in range(6)],
            rep=[sb(f"rep{i}", [128, T]) for i in range(4)],
            rope=sb("rope", [128, 2, T]),
            mod=sb("mod", [128, 2, 48]),
            sm=sb("sm", [128, 128]),
            sm16=sb("sm16", [16, 4 * T]),
            sc=sb("sc", [128, 384]),
            silu_c=sb("silu_c", [128, 8]),
            pos=sb("pos", [128, T + 2], I32),
            ps=[ctx.enter_context(nc.psum_tensor(f"ps{i}", [128, 512], F32)) for i in range(8)],
        )
        sems = {n: ctx.enter_context(nc.semaphore("s_" + n)) for n in
                ["pe", "act", "dve", "pool", "sp", "const", "x", "pos", "out"] + [f"raw{i}" for i in range(NRAW)]}
        plan = Program(nc, mem, sems, None, cst, posr, xin, out, dbg)
        plan.run()
        pieces = plan.W.pieces
        width = sum(wd for _, wd, _ in pieces)
        prog = Program(nc, mem, sems, pieces, cst, posr, xin, out, dbg)
        prog.wdram = w_stream_of(width)
        prog.run()
        block = ctx.enter_context(nc.Block())
        block.sync(prog.sp.play)
        block.scalar(prog.act.play)
        block.vector(prog.dve.play)
        block.gpsimd(prog.pool.play)
        block.tensor(prog.pe.play)
    return [(blocks, wd) for blocks, wd, _ in pieces]


class Weights:

    def __init__(self, p, pieces):
        self.p, self.known, self.pieces, self.i = p, pieces, [], 0
        self.split = {}
        self.used = {}
        self.lowers = "D"
        if pieces is not None:
            self.off = np.cumsum([0] + [wd for _, wd, _ in pieces]).tolist()
            self.loaded = {}
            for i in range(NRAW):
                self.load(i, [])
            for i in range(LOOK):
                self.make(i)

    def load(self, i, toks):
        if i >= len(self.known):
            return
        p, a, b, s = self.p, self.off[i], self.off[i + 1], i % NRAW
        self.loaded[i] = p.sp.dma(lambda e: e.dma_start(p.m["raw"][s][:, 0:b - a], p.wdram[:, a:b]),
                                  p.s[f"raw{s}"], 16 * (i // NRAW + 1), toks)

    def raw(self, i):
        return self.p.m["raw"][i % NRAW][:, 0:self.known[i][1]]

    def make(self, i):
        if i >= len(self.known) or self.known[i][2]:
            return
        p, wd, s = self.p, self.known[i][1], i % NHL
        raw, hi, lo = self.raw(i), p.m["wh"][s][:, 0:wd], p.m["wl"][s][:, 0:wd]
        free = self.used.get(i - NHL)
        th = p.act.do(lambda e: e.copy(hi, raw), self.loaded[i], free)
        eng = p.pool if self.lowers[i % len(self.lowers)] == "P" else p.dve
        tl = eng.do(lambda e: e.tensor_tensor(lo, raw, hi.bitcast(F32), ALU.subtract), self.loaded[i], th, free)
        self.split[i] = [th, tl]
        self.load(i + NRAW, [th, tl])

    def take(self, blocks, plain=False):
        i = self.i
        self.i += 1
        wd = sum(b[5] for b in blocks)
        self.pieces.append((blocks, wd, plain))
        if self.known is None:
            m = self.p.m
            return m["wh"][0][:, 0:wd] if not plain else m["raw"][0][:, 0:wd], m["wl"][0][:, 0:wd], []
        if plain:
            return self.raw(i), None, [self.loaded[i]]
        s = i % NHL
        return self.p.m["wh"][s][:, 0:wd], self.p.m["wl"][s][:, 0:wd], self.split[i]

    def done(self, tok):
        i = self.i - 1
        self.used[i] = tok
        if self.known is None:
            return
        if self.known[i][2]:
            self.load(i + NRAW, [tok])
        self.make(i + LOOK)


def cols(name, layer, c0, n=128, kt=8):
    return [(name, layer, 128 * k, 128, c0, n) for k in range(kt)]


class Program:
    def __init__(self, nc, mem, sems, pieces, cst, posr, xin, out, dbg):
        self.nc, self.m, self.s = nc, mem, sems
        self.cst, self.posr, self.xin, self.out, self.dbg = cst, posr, xin, out, dbg
        self.pe, self.act, self.dve, self.pool, self.sp = (Eng(sems[n]) for n in ("pe", "act", "dve", "pool", "sp"))
        self.wdram = None
        self.known = pieces
        self.bank = [Buf(b[:]) for b in mem["ps"]]
        self.tmp = Ring([t[:] for t in mem["t"]])
        self.osr = Ring([t[:] for t in mem["os"]])
        self.X = mem["X"]
        self.XS = mem["XS"]
        self.xt = [None] * 8
        self.xs_t = [None] * 8
        self.xs_free = []
        self.bfree = [[] for _ in range(4)]
        self.background = []
        self.ndbg = 0

    def c(self, name, k=0, n=1, rows=slice(0, 128)):
        o = COFF[name][0] + k
        return self.m["C"][rows, o:o + n]

    def tt(self, o, a, b, op, *w, eng=None):
        return (eng or self.dve).do(lambda e: e.tensor_tensor(o, a, b, op), *w)

    def ts(self, o, a, s1, s2, op0, op1, *w, eng=None):
        if op1 is None:
            return (eng or self.dve).do(lambda e: e.tensor_scalar(o, a, s1, None, op0), *w)
        return (eng or self.dve).do(lambda e: e.tensor_scalar(o, a, s1, s2, op0, op1), *w)

    def stt(self, o, a, s, b, op0, op1, *w):
        return self.dve.do(lambda e: e.scalar_tensor_tensor(out=o, in0=a, scalar=s, in1=b, op0=op0, op1=op1), *w)

    def cp(self, o, a, *w):
        return self.dve.do(lambda e: e.tensor_copy(o, a), *w)

    def fn(self, o, a, f, *w, **kw):
        return self.act.do(lambda e: e.activation(o, a, f, **kw), *w)

    def mms(self, group, *w, skip=False):
        self.pe.wait(*w)
        for n, (o, a, b, st, sp) in enumerate(group):
            f = (lambda e, o=o, a=a, b=b, st=st, sp=sp: e.matmul(o, a, b, start=st, stop=sp, skip_group_check=skip)
                 if skip else e.matmul(o, a, b, start=st, stop=sp))
            if n == len(group) - 1:
                return self.pe.do(f)
            self.pe.quiet(f)

    def some_background(self, n=1):
        for _ in range(n):
            if self.background:
                self.background.pop(0)()

    def xh(self, k):
        return self.XS[:, k, 0:T]

    def xl(self, k):
        return self.XS[:, k, T:2 * T]

    def split_pairs(self, kt, hi, lo, W, M):
        g = []
        for k in range(kt):
            wh, wl = W[0][:, k * M:(k + 1) * M], W[1][:, k * M:(k + 1) * M]
            g += [(wh, hi(k)), (wh, lo(k)), (wl, hi(k))]
        return g

    def unit(self, out, blocks, *w, M=128, kt=8):
        W = self.W.take(blocks)
        g = self.split_pairs(kt, self.xh, self.xl, W, M)
        tok = self.mms([(out, a, b, n == 0, n == len(g) - 1) for n, (a, b) in enumerate(g)], W[2], self.xs_t, *w)
        self.W.done(tok)
        return tok

    def pair(self, bank, name, layer, c0, c1, *w):
        b = self.bank[bank]
        self.unit(b.ap[:, 0:T], cols(name, layer, c0), b.free, *w)
        return self.unit(b.ap[:, T:2 * T], cols(name, layer, c1))

    def token_major(self, banks, name, layer, c0, n=512, colmap=None):
        for kp in range(4):
            blocks = []
            for k in (2 * kp, 2 * kp + 1):
                if colmap is None:
                    blocks.append((name, layer, 128 * k, 128, c0, n))
                else:
                    blocks += [(name, layer, 128 * k, 128, a, m) for a, m in colmap]
            W = self.W.take(blocks)
            for tb in range(2):
                tk = slice(tb * 128, tb * 128 + 128)
                tl = slice(T + tb * 128, T + tb * 128 + 128)
                o = self.bank[banks[tb]].ap[:, 0:n]
                g = []
                for kk in range(2):
                    k = 2 * kp + kk
                    wh, wl = W[0][:, kk * n:(kk + 1) * n], W[1][:, kk * n:(kk + 1) * n]
                    g += [(self.XS[:, k, tk], wh), (self.XS[:, k, tl], wh), (self.XS[:, k, tk], wl)]
                tok = self.mms([(o, a, b, kp == 0 and i == 0, kp == 3 and i == 5) for i, (a, b) in enumerate(g)],
                               W[2], self.xs_t, self.bank[banks[tb]].free if kp == 0 else None, skip=True)
            self.W.done(tok)
        return tok

    def split_out(self, src, *w):
        o = self.osr.take()
        th = self.act.do(lambda e: e.copy(o.ap[:, 0:T], src), *w, o.free)
        tl = self.tt(o.ap[:, T:2 * T], src, o.ap[:, 0:T].bitcast(F32), ALU.subtract, *w, th)
        return o, [th, tl]

    def out_k(self, k, K, name, layer, hi, lo, *w):
        W = self.W.take([(name, layer, 128 * k, 128, 0, D)])
        g = []
        for m in range(8):
            o = self.bank[m // 2].ap[:, (m % 2) * T:(m % 2) * T + T]
            wh, wl = W[0][:, m * 128:(m + 1) * 128], W[1][:, m * 128:(m + 1) * 128]
            g += [(o, wh, hi, k == 0 and m % 2 == 0, False), (o, wh, lo, False, False),
                  (o, wl, hi, False, k == K - 1)]
        tok = self.mms(g, W[2], *w, [self.bank[i].free for i in range(4)] if k == 0 else None, skip=True)
        self.W.done(tok)
        return tok

    def residual(self, tok):
        for i in range(4):
            o = self.X[:, 2 * i:2 * i + 2, :]
            s = self.bank[i].ap.rearrange("p (a t) -> p a t", a=2)
            t = self.tt(o, o, s, ALU.add, tok, self.xt)
            self.bank[i].free = [t]
            self.xt_new = t
        self.xt = [t] * 8
        self.dump()

    def dump(self):
        if self.dbg is not None:
            k = self.ndbg
            t = self.sp.dma(lambda e: e.dma_start(self.dbg[k], self.X[:]), self.s["out"], 16 * (k + 1), self.xt)
            self.xt = self.xt + [t]
        self.ndbg += 1

    def inv_sqrt(self, o, v, src, n, eps, *w, tmp):
        t = self.ts(v, src, 1.0 / n, eps, ALU.mult, ALU.add, *w)
        return self.root(o, v, tmp, t), t

    def root(self, o, v, tmp, *w):
        t = self.fn(tmp, v, ACT.Sqrt, *w)
        t = self.dve.do(lambda e: e.reciprocal(o, tmp), t)
        t = self.tt(tmp, o, o, ALU.mult, t)
        t = self.stt(tmp, tmp, -0.5, v, ALU.mult, ALU.mult, t)
        return self.stt(o, tmp, 1.5, o, ALU.add, ALU.mult, t)

    def sum_tiles(self, bank, tiles, toks, square):
        b = self.bank[bank]
        ones = self.c("ones", 0, 128)
        n = len(tiles)
        for i, (a, w) in enumerate(zip(tiles, toks)):
            src, tw = a, w
            if square:
                q = self.tmp.take()
                src = q.ap[:, 0:T]
                tw = self.fn(src, a, ACT.Square, w, q.free)
            tok = self.mms([(b.ap[:, 0:T], ones, src, i == 0, i == n - 1)], tw, b.free if i == 0 else None)
            if square:
                q.release([tok])
        return tok

    def rms_in(self, gname):
        xn = self.m["B"][3][:, 0:2048].rearrange("p (a t) -> p a t", a=8)
        tok = self.sum_tiles(7, [self.X[:, m, :] for m in range(8)], self.xt, True)
        R, v, s = self.m["rep"][0][:], self.m["rep"][1][:], self.m["rep"][2][:]
        t, tv = self.inv_sqrt(R, v, self.bank[7].ap[:, 0:T], D, 1e-6, tok, tmp=s)
        self.bank[7].free = [tv]
        for i in range(4):
            a = slice(2 * i, 2 * i + 2)
            t1 = self.tt(xn[:, a, :], self.X[:, a, :], R.unsqueeze(1).to_broadcast([128, 2, T]), ALU.mult,
                         t, self.bfree[3])
            for m in (2 * i, 2 * i + 1):
                g = self.c(gname, m)
                th = self.fn(self.xh(m), xn[:, m, :], ACT.Identity, t1, self.xs_free, scale=g)
                tl = self.stt(self.xl(m), xn[:, m, :], g, self.xh(m).bitcast(F32), ALU.mult, ALU.subtract, th)
                self.xs_t[m] = [th, tl]
        self.bfree[3] = [tl, th]

    def layer_a(self, j):
        m, c = self.m, self.c
        self.rms_in(f"a_norm{j}")
        self.W.lowers = "P"
        U = m["B"][3][:, 2048:4096].rearrange("p (i t) -> p i t", i=8)
        A = m["B"][1][:].rearrange("p (i t) -> p i t", i=16)
        Z = m["B"][2][:].rearrange("p (i t) -> p i t", i=16)
        ones = c("ones", 0, 128)
        ut, at, sq, tz = {}, {}, {}, []
        w_conv, b_conv = f"a_conv_w{j}", f"a_conv_b{j}"

        def conv_step(i, k):
            u = U[:, i % 8, :]
            if k == 30:
                at[i] = self.fn(A[:, i, :], u, ACT.Identity, ut[i // 2], self.bfree[1],
                                scale=c(w_conv, 30 * 16 + i), bias=c(b_conv, i))
            else:
                s = 30 - k
                at[i] = self.stt(A[:, i, s:T], u[:, 0:T - s], c(w_conv, k * 16 + i), A[:, i, s:T],
                                 ALU.mult, ALU.add, ut[i // 2], at[i])

        def stats(i):
            q = self.tmp.take()
            tq = self.fn(q.ap[:, 0:T], A[:, i, :], ACT.Square, at[i], q.free)
            self.mms([(self.bank[2].ap[:, 0:T], ones, A[:, i, :], i == 0, i == 15)], at[i], self.bank[2].free)
            sq[i] = self.mms([(self.bank[3].ap[:, 0:T], ones, q.ap[:, 0:T], i == 0, i == 15)], tq, self.bank[3].free)
            q.release([sq[i]])

        todo = []

        def convolve(n):
            for _ in range(n):
                if todo:
                    todo.pop(0)()

        for i in range(0, 16, 2):
            bv, bg, bz = (4 + (3 * i // 2 + n) % 4 for n in range(3))
            tg = self.pair(bg, "a_w_in", j, E + i * 128, E + i * 128 + 128)
            sg = self.tmp.take()
            t1 = self.fn(sg.ap, self.bank[bg].ap, ACT.Sigmoid, tg, sg.free)
            self.bank[bg].free = [t1]
            convolve(8)
            tv = self.pair(bv, "a_w_in", j, i * 128, i * 128 + 128)
            while i >= 8 and i - 7 not in sq:
                convolve(1)
            a = i % 8
            ut[i // 2] = self.tt(U[:, a:a + 2, :].rearrange("p a t -> p (a t)"), self.bank[bv].ap, sg.ap, ALU.mult,
                                 tv, t1, self.bfree[3])
            self.bank[bv].free = [ut[i // 2]]
            sg.release([ut[i // 2]])
            for k in range(30, -1, -1):
                todo.append(lambda i=i, k=k: (conv_step(i, k), conv_step(i + 1, k)))
            todo.append(lambda i=i: (stats(i), stats(i + 1)))
            convolve(9)
            t = self.pair(bz, "a_w_in", j, 2 * E + i * 128, 2 * E + i * 128 + 128)
            t = self.fn(Z[:, i:i + 2, :].rearrange("p a t -> p (a t)"), self.bank[bz].ap, ACT.Silu, t, self.bfree[2])
            self.bank[bz].free = [t]
            tz.append(t)
            convolve(9)
        self.xs_free = [(self.pe.sem, self.pe.n)]
        while todo:
            if len(todo) % 2 == 0:
                self.ada(1)
            convolve(1)
        self.ada(8)
        self.W.lowers = "D"
        mu, v, s, R = (m["rep"][i][:] for i in range(4))
        t1 = self.ts(mu, self.bank[2].ap[:, 0:T], 1.0 / E, None, ALU.mult, None, sq[15])
        t2 = self.ts(v, self.bank[3].ap[:, 0:T], 1.0 / E, 1e-6, ALU.mult, ALU.add, sq[15])
        self.bank[2].free, self.bank[3].free = [t1], [t2]
        t3 = self.tt(s, mu, mu, ALU.mult, t1)
        t4 = self.tt(v, v, s, ALU.subtract, t3, t2)
        tr = self.root(R, v, s, t4)
        for i in range(0, 16, 2):
            a = A[:, i:i + 2, :]
            bc = mu.unsqueeze(1).to_broadcast([128, 2, T])
            t = self.tt(a, a, bc, ALU.subtract, at[i], at[i + 1], sq[i], sq[i + 1], t1)
            t = self.tt(a, a, R.unsqueeze(1).to_broadcast([128, 2, T]), ALU.mult, t, tr)
            for k in (i, i + 1):
                ts = self.fn(A[:, k, :], A[:, k, :], ACT.Silu, t, scale=c(f"a_ln_g{j}", k), bias=c(f"a_ln_b{j}", k))
                tm = self.tt(A[:, k, :], A[:, k, :], Z[:, k, :], ALU.mult, ts, tz[i // 2])
                o, w = self.split_out(A[:, k, :], tm)
                tok = self.out_k(k, 16, "a_w_out", j, o.ap[:, 0:T], o.ap[:, T:2 * T], w)
                o.release([tok])
        self.bfree[3] = [tr]
        self.bfree[1] = [w[0], w[1]]
        self.bfree[2] = [tm]
        self.residual(tok)

    def layer_b(self):
        m, c = self.m, self.c
        self.rms_in("b_norm")
        K = m["B"][0][:].rearrange("p (i t) -> p i t", i=16)
        Q = m["B"][1][:].rearrange("p (i t) -> p i t", i=16)
        Z = m["B"][2][:].rearrange("p (i t) -> p i t", i=16)
        V = m["B"][3][:].rearrange("p (b e) -> p b e", b=2)
        I16 = c("ident", 0, 16, rows=slice(0, 16))
        b = self.bank[4]
        tf = self.unit(b.ap[:, 0:T], cols("b_w_in", 0, 4 * E - 112), b.free)
        tb = self.tmp.take()
        f = tb.ap[:, 0:T]
        t = self.fn(f, b.ap[:, 0:T], ACT.Identity, tf, tb.free)
        b.free = [t]
        b6 = self.bank[6]
        t = self.mms([(b6.ap[0:16, 0:T], c("ident", 112, 16), f, True, True)], t, b6.free)
        tb.release([t])
        y, e1, lf, cc, ncs = (self.m["rep"][1][0:16, :], self.m["rep"][2][0:16, :], self.m["rep"][3][0:16, :],
                              self.m["sm16"][0:16, 0:T], self.m["sm16"][0:16, T:2 * T])
        t = self.ts(y, b6.ap[0:16, 0:T], c("b_f_bias", 0, 1, rows=slice(0, 16)), None, ALU.add, None, t)
        b6.free = [t]
        ta = self.fn(e1, y, ACT.Abs, t)
        ta = self.fn(e1, e1, ACT.Exp, ta, scale=-1.0)
        ta = self.fn(e1, e1, ACT.Ln, ta, bias=1.0)
        t = self.stt(lf, y, 0.0, e1, ALU.min, ALU.subtract, t, ta)
        t = self.dve.do(lambda e: e.tensor_tensor_scan(out=cc, data0=self.c("ones", 0, 128, rows=slice(0, 16))[:, 0:1]
                                                       .to_broadcast([16, T]), data1=lf, initial=0.0,
                                                       op0=ALU.mult, op1=ALU.add), t)
        tn = self.ts(ncs, cc, -1.0, None, ALU.mult, None, t)
        ct = m["sm"][:, 0:32]
        g = [(b6.ap[:, 16 * k:16 * k + 16], cc[:, 128 * k:128 * k + 128], I16, True, True) for k in range(2)]
        tp = self.mms(g, t, b6.free)
        tct = self.cp(ct, b6.ap[:, 0:32], tp)
        b6.free = [tct]
        tv = []
        for n in range(4):
            banks = (4, 5) if n % 2 == 0 else (6, 7)
            tok = self.token_major(banks, "b_w_in", 0, 2 * E + 512 * n)
            for k in range(2):
                bb = self.bank[banks[k]]
                o = V[:, k, 512 * n:512 * n + 512]
                t = self.fn(o, bb.ap, ACT.Identity, tok, self.bfree[3]) if k else self.cp(o, bb.ap, tok, self.bfree[3])
                bb.free = [t]
                tv.append(t)
        rows = {}
        for which, (dst, base, sbank, bf) in enumerate(((K, E, 0, 0), (Q, 0, 1, 1))):
            kt = []
            ss = self.bank[sbank]
            for n, i in enumerate(range(0, 16, 2)):
                bb = self.bank[4 + n % 4]
                t = self.pair(4 + n % 4, "b_w_in", 0, base + i * 128, base + i * 128 + 128)
                q = self.tmp.take()
                t1 = self.fn(dst[:, i:i + 2, :].rearrange("p a t -> p (a t)"), bb.ap, ACT.Identity, t, self.bfree[bf])
                t2 = self.fn(q.ap, bb.ap, ACT.Square, t, q.free)
                bb.free = [t1, t2]
                kt.append(t1)
                for k in range(2):
                    h = i + k
                    ts = self.mms([(ss.ap[0:16, 0:T], c("onehot", 15 - h, 16), q.ap[:, k * T:k * T + T],
                                    h == 0, h == 15)], t2, ss.free if h == 0 else None)
                q.release([ts])
            r = self.m["sm16"][0:16, (2 + which) * T:(3 + which) * T]
            v, s = m["rep"][1][0:16, :], m["rep"][2][0:16, :]
            t, tv_ = self.inv_sqrt(r, v, ss.ap[0:16, 0:T], 128, 1e-6, ts, tmp=s)
            ss.free = [tv_]
            if which:
                t = self.ts(r, r, 128.0 ** -0.5, None, ALU.mult, None, t)
            rows[which] = (r, t, kt)
        tz = []
        for n, i in enumerate(range(0, 16, 2)):
            b = self.bank[4 + n % 4]
            t = self.pair(4 + n % 4, "b_w_in", 0, 3 * E + i * 128, 3 * E + i * 128 + 128)
            t = self.fn(Z[:, i:i + 2, :].rearrange("p a t -> p (a t)"), b.ap, ACT.Silu, t, self.bfree[2])
            b.free = [t]
            tz.append(t)
        self.xs_free = [(self.pe.sem, self.pe.n)]
        ctr = ct.rearrange("p (b h) -> p b h", b=2)
        ready, tail = {}, {}

        def scale_qk(h):
            b = self.bank[4]
            sel = I16[:, h:h + 1].to_broadcast([16, 128])
            t = self.mms([(b.ap[:, 0:T], sel, rows[0][0], True, True), (b.ap[:, T:2 * T], sel, rows[1][0], True, True)],
                         rows[0][1], rows[1][1], b.free)
            t1 = self.stt(K[:, h, :], K[:, h, :], c("b_k_norm"), b.ap[:, 0:T], ALU.mult, ALU.mult, t, rows[0][2][h // 2])
            t2 = self.stt(Q[:, h, :], Q[:, h, :], c("b_q_norm"), b.ap[:, T:2 * T], ALU.mult, ALU.mult, t,
                          rows[1][2][h // 2])
            b.free = [t2]
            ready[h] = [t1, t2]

        def scores(h):
            b = self.bank[5]
            sel = I16[:, h:h + 1].to_broadcast([16, 128])
            idn, tri = c("ident", 0, 128), c("cmask", 0, 128)
            o0, o1, o1d = b.ap[:, 0:128], b.ap[:, 128:384], b.ap[:, 256:384]
            t = self.mms([(o0, Q[:, h, 0:128], K[:, h, 0:128], True, False), (o0, sel, ncs[:, 0:128], False, False),
                          (o0, idn, tri, False, True),
                          (o1, Q[:, h, 128:256], K[:, h, :], True, False), (o1, sel, ncs, False, False),
                          (o1d, idn, tri, False, True)], ready[h], tn, b.free)
            st = self.stat(h)
            t1 = self.red(st[:, 0:1], o0, t)
            t2 = self.red(st[:, 1:2], o1, t)
            t3 = self.tt(st[:, 2:4], st[:, 0:2], ctr[:, :, h], ALU.add, t1, t2, tct)
            t4 = self.tt(st[:, 2:4], ctr[:, :, h], st[:, 2:4], ALU.subtract, t3)
            pt = self.exps(h, o0, o1, st, 1.0, t4)
            b.free = [pt[1]]
            tail[h] = pt[0]

        def value(h):
            t = self.turn(h, tail[h])
            t, pv = self.pv(h, V[:, 0, h * 128:h * 128 + 128], V[:, 1, h * 128:h * 128 + 128], t, tv, slice(0, 128))
            q = self.tmp.take()
            t = self.tt(q.ap[:, 0:T], self.bank[7].ap[:, 0:T], Z[:, h, :], ALU.mult, t, tz[h // 2], q.free)
            self.bank[7].free = [t]
            o, w = self.split_out(q.ap[:, 0:T], t)
            q.release(w)
            outs[h] = (o, w)

        outs = {}
        for s in range(16 + 3):
            if s < 16:
                scale_qk(s)
            if 0 <= s - 2 < 16:
                value(s - 2)
            if 0 <= s - 1 < 16:
                scores(s - 1)
            if s >= 3:
                h = s - 3
                o, w = outs[h]
                tok = self.out_k(h, 16, "b_w_out", 0, o.ap[:, 0:T], o.ap[:, T:2 * T], w)
                o.release([tok])
        fin = [tok, w[1]]
        self.bfree = [fin, fin, fin, fin]
        self.residual(tok)

    def stat(self, h):
        k = 32 + 8 * (h % 4)
        return self.m["sm"][:, k:k + 8]

    def red(self, o, a, *w):
        return self.dve.do(lambda e: e.tensor_reduce(o, a, AX, ALU.max), *w)

    def exps(self, h, s0, s1, st, scale, *w):
        P = self.tmp.take()
        ta = self.fn(P.ap[:, 0:128], s0, ACT.Exp, *w, P.free, bias=st[:, 2:3], scale=scale, accum_out=st[:, 4:5])
        tb = self.fn(P.ap[:, 128:384], s1, ACT.Exp, *w, bias=st[:, 3:4], scale=scale, accum_out=st[:, 5:6])
        t = self.dve.do(lambda e: e.reciprocal(st[:, 6:8], st[:, 4:6]), ta, tb)
        t1 = self.ts(P.ap[:, 0:128], P.ap[:, 0:128], st[:, 6:7], None, ALU.mult, None, t)
        t2 = self.ts(P.ap[:, 128:384], P.ap[:, 128:384], st[:, 7:8], None, ALU.mult, None, t)
        return (P, [t1, t2]), tb

    def turn(self, h, tail):
        P, w = tail
        b = self.bank[6]
        idn = self.c("ident", 0, 128)
        self.pe.wait(w, b.free)
        for k in range(3):
            a, o = P.ap[:, 128 * k:128 * k + 128], b.ap[:, 128 * k:128 * k + 128]
            f = lambda e, a=a, o=o: e.transpose(o, a, idn)
            if k < 2:
                self.pe.quiet(f)
            else:
                t = self.pe.do(f)
        t = self.fn(P.ap[:, 0:384], b.ap[:, 0:384], ACT.Identity, t)
        b.free = [t]
        self.turned = P
        return t

    def pv(self, h, v0, v1, t, tv, part, bank=7, first=True):
        b, P = self.bank[bank], self.turned
        t = self.mms([(b.ap[part, 0:T], v0, P.ap[:, 0:T], True, False),
                      (b.ap[part, 128:T], v1, P.ap[:, 256:384], False, True)], t, tv, b.free if first else None)
        P.release([t])
        return t, P

    def layer_c(self):
        m, c = self.m, self.c
        self.rms_in("c_norm")
        outs = {}

        def emit_out(k):
            o, w = outs[k]
            tok = self.out_k(k, 16, "c_w_out", 0, o.ap[:, 0:T], o.ap[:, T:2 * T], w)
            o.release([tok])
            return tok

        for i in range(0, 16, 2):
            tk = self.pair(4, "c_w_in", 0, 2 * E + i * 128, 2 * E + i * 128 + 128)
            cs = self.tmp.take()
            t = self.fn(cs.ap, self.bank[4].ap, ACT.Identity, tk, cs.free)
            self.bank[4].free = [t]
            tk = self.pair(5, "c_w_in", 0, i * 128, i * 128 + 128)
            tcu = self.tt(cs.ap, self.bank[5].ap, cs.ap, ALU.mult, tk, t)
            self.bank[5].free = [tcu]
            ac = self.tmp.take()
            tk = self.pair(6, "c_w_in", 0, E + i * 128, E + i * 128 + 128)
            ta = []
            for k in range(2):
                a, u = ac.ap[:, k * T:k * T + T], cs.ap[:, k * T:k * T + T]
                ta.append(self.fn(a, u, ACT.Identity, tcu, ac.free, scale=c("c_conv_w", 32 + i + k)))
            for s in (1, 2):
                for k in range(2):
                    a, u = ac.ap[:, k * T + s:k * T + T], cs.ap[:, k * T:k * T + T - s]
                    ta[k] = self.stt(a, u, c("c_conv_w", (2 - s) * 16 + i + k), a, ALU.mult, ALU.add, ta[k])
            t = self.tt(ac.ap, self.bank[6].ap, ac.ap, ALU.mult, tk, ta)
            self.bank[6].free = [t]
            cs.release([t])
            if i >= 2:
                emit_out(i - 2)
            tk = self.pair(7, "c_w_in", 0, 3 * E + i * 128, 3 * E + i * 128 + 128)
            if i >= 2:
                emit_out(i - 1)
            zs = self.tmp.take()
            tz = self.fn(zs.ap, self.bank[7].ap, ACT.Silu, tk, zs.free)
            self.bank[7].free = [tz]
            t = self.tt(ac.ap, ac.ap, zs.ap, ALU.mult, t, tz)
            zs.release([t])
            for k in range(2):
                outs[i + k] = self.split_out(ac.ap[:, k * T:k * T + T], t)
            ac.release(outs[i][1] + outs[i + 1][1])
            self.some_background(26)
        self.xs_free = [(self.pe.sem, self.pe.n)]
        emit_out(14)
        tok = emit_out(15)
        self.residual(tok)

    def ada(self, n):
        while n > 0 and self.ada_i < 96:
            l, u0 = divmod(self.ada_i, 48)
            u1 = min(48, u0 + n)
            b = self.bank[0]
            for u in range(u0, u1):
                W = self.W.take(cols("w_ada_2", l, 128 * u), plain=True)
                tok = self.mms([(b.ap[:, u:u + 1], W[0][:, k * 128:(k + 1) * 128], self.m["silu_c"][:, k:k + 1],
                                 k == 0, k == 7) for k in range(8)], W[2], self.silu_t, b.free)
                self.W.done(tok)
            self.ada_i += u1 - u0
            n -= u1 - u0
            md = self.m["mod"][:, l, :]
            t = self.tt(md[:, u0:u1], b.ap[:, u0:u1], self.c(f"b_ada{l}", u0, u1 - u0), ALU.add, tok)
            b.free = [t]
            self.mod_t[l].append(t)
            if u1 == 48:
                for a in (8, 32):
                    self.mod_t[l].append(self.ts(md[:, a:a + 8], md[:, a:a + 8], 1.0, None, ALU.add, None,
                                                 self.mod_t[l]))

    def modulate(self, l, which):
        md = self.m["mod"][:, l, :]
        sh, sc = (0, 8) if which == 0 else (24, 32)
        for k in range(8):
            q = self.tmp.take()
            t = self.fn(q.ap[:, 0:T], self.X[:, k, :], ACT.Identity, self.xt[k], self.mod_t[l], q.free,
                        scale=md[:, sc + k:sc + k + 1], bias=md[:, sh + k:sh + k + 1])
            th = self.act.do(lambda e, k=k, q=q: e.copy(self.xh(k), q.ap[:, 0:T]), t, self.xs_free)
            tl = self.tt(self.xl(k), q.ap[:, 0:T], self.xh(k).bitcast(F32), ALU.subtract, t, th, self.xs_free)
            q.release([tl, th])
            self.xs_t[k] = [th, tl]

    def post_norm(self, l, which, tok):
        md = self.m["mod"][:, l, :]
        g = 16 if which == 0 else 40
        n = "ln1" if which == 0 else "ln2"
        b6, b7 = self.bank[6], self.bank[7]
        ones = self.c("ones", 0, 128)
        for k in range(8):
            x = self.X[:, k, :]
            t = self.fn(x, x, ACT.Identity, self.xt[k], self.xs_t, scale=ALPHA)
            b = self.bank[k // 2]
            t = self.stt(x, b.ap[:, (k % 2) * T:(k % 2) * T + T], md[:, g + k:g + k + 1], x, ALU.mult, ALU.add,
                         t, tok, self.mod_t[l])
            b.free = [t]
            self.xt[k] = t
            q = self.tmp.take()
            tq = self.fn(q.ap[:, 0:T], x, ACT.Square, t, q.free)
            self.mms([(b6.ap[:, 0:T], ones, x, k == 0, k == 7)], t, b6.free if k == 0 else None)
            t = self.mms([(b7.ap[:, 0:T], ones, q.ap[:, 0:T], k == 0, k == 7)], tq, b7.free if k == 0 else None)
            q.release([t])
        mu, v, s, R = (self.m["rep"][i][:] for i in range(4))
        t1 = self.ts(mu, b6.ap[:, 0:T], 1.0 / D, None, ALU.mult, None, t)
        t2 = self.ts(v, b7.ap[:, 0:T], 1.0 / D, 1e-5, ALU.mult, ALU.add, t)
        b6.free, b7.free = [t1], [t2]
        t3 = self.tt(s, mu, mu, ALU.mult, t1)
        t4 = self.tt(v, v, s, ALU.subtract, t3, t2)
        tr = self.root(R, v, s, t4)
        for i in range(4):
            a = self.X[:, 2 * i:2 * i + 2, :]
            u = self.tt(a, a, mu.unsqueeze(1).to_broadcast([128, 2, T]), ALU.subtract, t, t1, self.xt)
            u = self.tt(a, a, R.unsqueeze(1).to_broadcast([128, 2, T]), ALU.mult, u, tr)
            for k in (2 * i, 2 * i + 1):
                self.xt[k] = self.fn(self.X[:, k, :], self.X[:, k, :], ACT.Identity, u,
                                     scale=self.c(f"{n}_g{l}", k), bias=self.c(f"{n}_b{l}", k))
        self.dump()

    def make_bias(self):
        m, c = self.m, self.c
        Bz = m["B"][0][:, 0:8 * 384].rearrange("p (h s) -> p h s", h=8)
        n = m["B"][2][:, 0:384]
        bk = m["B"][2][:, 384:768]
        eq = [m["B"][2][:, 768:1152], m["B"][2][:, 1152:1536]]
        pf = m["B"][2][:, 1536:1536 + T + 2]
        st = {}
        back = self.background

        def start():
            t = self.cp(pf, m["pos"][:], self.tpos, self.bfree[2])
            for o, k, w in ((0, 0, 128), (128, 1, 256)):
                st["n%d" % k] = self.ts(n[:, o:o + w], pf[:, 0:w], pf[:, T + k:T + k + 1], -1.0, ALU.subtract,
                                        ALU.mult, t)
            t = self.ts(n, n, 0.0, None, ALU.max, None, st["n0"], st["n1"])
            st["n"] = t
            st["b"] = self.ts(bk, n, 15.0, None, ALU.min, None, t)
        back.append(start)
        for thr in bucket_starts():
            def step(thr=thr):
                st["b"] = self.stt(bk, n, float(thr), bk, ALU.is_ge, ALU.add, st["n"], st["b"])
            back.append(step)
        for b in range(32):
            def mask(b=b):
                st["m", b] = self.ts(eq[b % 2], bk, float(b), None, ALU.is_equal, None, st["b"], st.get(("u", b - 2)))
            back.append(mask)
            for h in range(8):
                def add(b=b, h=h):
                    r = c("rel_bias", b * 8 + h)
                    if b == 0:
                        t = self.ts(Bz[:, h, :], eq[0], r, None, ALU.mult, None, st["m", 0], self.bfree[0])
                    else:
                        t = self.stt(Bz[:, h, :], eq[b % 2], r, Bz[:, h, :], ALU.mult, ALU.add, st["m", b],
                                     st["h", h])
                    st["h", h] = t
                    st["u", b] = t
                back.append(add)

        def finish():
            self.bias_t = [st["h", h] for h in range(8)]
            self.bfree[2] = self.bias_t
        back.append(finish)
        self.Bz = Bz

    def make_rope(self):
        m, c = self.m, self.c
        r = slice(64, 96)
        C, S = m["rope"][:, 0, :], m["rope"][:, 1, :]
        q, q2 = self.tmp.take(), self.tmp.take()
        a, k, w, pf = q.ap[r, 0:T], q.ap[r, T:2 * T], q2.ap[r, 0:T], q2.ap[r, T:2 * T]
        t0 = self.dve.do(lambda e: e.memset(m["rope"][0:64, 0, :], 1.0))
        t00 = self.dve.do(lambda e: e.memset(m["rope"][0:64, 1, :], 0.0))
        t = self.cp(pf, m["pos"][r, 0:T], self.tpos, q2.free, q.free)
        t = self.ts(a, pf, c("freq", 0, 1, rows=r), None, ALU.mult, None, t, self.tconst)
        t = self.ts(k, a, 1.0 / (2 * math.pi), MAGIC, ALU.mult, ALU.add, t)
        t = self.ts(k, k, -MAGIC, None, ALU.add, None, t)
        for part in TWO_PI:
            t = self.stt(a, k, -part, a, ALU.mult, ALU.add, t)
        t = self.ts(a, a, 3.1415925, -3.1415925, ALU.min, ALU.max, t)
        ts = self.fn(S[r, :], a, ACT.Sin, t)
        t = self.ts(w, a, -1.0, None, ALU.mult, None, t)
        t = self.tt(w, w, a, ALU.max, t)
        t = self.ts(w, w, -1.0, math.pi / 2, ALU.mult, ALU.add, t)
        tc = self.fn(C[r, :], w, ACT.Sin, t)
        t = self.ts(S[r, :], S[r, :], c("ropemul", 0, 1, rows=r), None, ALU.mult, None, ts)
        q.release([tc, ts, t])
        q2.release([tc, ts, t])
        self.rope_t = [t0, t00, t, tc]

    def mixer(self, l):
        m, c = self.m, self.c
        self.modulate(l, 0)
        w = "w_in_2"
        o_iq, o_ik, o_iw, o_cq, o_ckv, o_kr, o_ga, o_gb = 1536, 2048, 2112, 2120, 2376, 2504, 2536, 3560
        B0 = m["B"][1]
        QA = B0[:, 0:1024].rearrange("p (i t) -> p i t", i=4)
        KA = B0[:, 1024:2048].rearrange("p (i t) -> p i t", i=4)
        IQ = B0[:, 2048:3072].rearrange("p (i t) -> p i t", i=4)
        VM = B0[:, 2048:3072].rearrange("p (b e) -> p b e", b=2)
        IK = B0[:, 3072:3328]
        CQ = B0[:, 3328:3840].rearrange("p (i t) -> p i t", i=2)
        CKV = B0[:, 3840:4096]
        GA = m["B"][3][:, 0:2048].rearrange("p (i t) -> p i t", i=8)
        GB = m["B"][3][:, 2048:4096].rearrange("p (i t) -> p i t", i=8)
        QM = m["B"][2][:, 0:2048].rearrange("p (i t) -> p i t", i=8)
        KM = m["B"][2][:, 2048:4096].rearrange("p (i t) -> p i t", i=8)
        VA = m["B"][0][:, 3072:4096].rearrange("p (b e) -> p b e", b=2)
        f0, f1, f2, f3 = self.bfree[1], self.bfree[0], self.bfree[2], self.bfree[3]
        bk = self.bank

        def ev(o, bank, *w, eng="a"):
            b = bk[bank]
            t = self.fn(o, b.ap[:, 0:o_size(o)], ACT.Identity, *w) if eng == "a" else self.cp(o, b.ap[:, 0:o_size(o)], *w)
            b.free = [t]
            return t

        def o_size(o):
            return o.shape[1] if len(o.shape) == 2 else o.shape[1] * o.shape[2]

        W = self.W.take([(w, l, 128 * k, 128, o_iw, 8) for k in range(8)])
        b = bk[4]
        g = []
        for tb in range(2):
            o = b.ap[:, 8 * tb:8 * tb + 8]
            tk, tl = slice(tb * 128, tb * 128 + 128), slice(T + tb * 128, T + tb * 128 + 128)
            for k in range(8):
                wh, wl = W[0][:, 8 * k:8 * k + 8], W[1][:, 8 * k:8 * k + 8]
                g += [(o, self.XS[:, k, tk], wh, k == 0, False), (o, self.XS[:, k, tl], wh, False, False),
                      (o, self.XS[:, k, tk], wl, False, k == 7)]
        t = self.mms(g, W[2], self.xs_t, b.free)
        self.W.done(t)
        iw = m["sm"][:, 64:80]
        tiw = self.ts(iw, b.ap[:, 0:16], 8.0 ** -0.5, None, ALU.mult, None, t, f0)
        b.free = [tiw]
        b = bk[5]
        t = self.unit(b.ap[:, 0:T], [x for k in range(8) for x in [(w, l, 128 * k, 128, o_ik, 64)] * 2], b.free)
        tik = ev(IK, 5, t, f0)
        tiq = []
        for n in range(2):
            t = self.pair(6 + n, w, l, o_iq + 256 * n, o_iq + 256 * n + 128)
            tiq.append(ev(IQ[:, 2 * n:2 * n + 2, :].rearrange("p a t -> p (a t)"), 6 + n, t, f0))
        sc = m["sc"][:]
        sct = [None]

        def index_head(h):
            b = bk[2 + h % 2]
            r = slice(64 * (h % 2), 64 * (h % 2) + 64)
            t = self.mms([(b.ap[:, 0:128], IQ[r, h // 2, 0:128], IK[r, 0:128], True, True),
                          (b.ap[:, 128:384], IQ[r, h // 2, 128:256], IK[r, :], True, True)], tik, tiq, b.free)
            q = self.tmp.take()
            t = self.fn(q.ap[:, 0:384], b.ap[:, 0:384], ACT.Relu, t, q.free, scale=0.125)
            b.free = [t]
            ts = []
            for o, k, wd in ((0, 0, 128), (128, 1, 256)):
                s = iw[:, 8 * k + h:8 * k + h + 1]
                if h == 0:
                    ts.append(self.ts(sc[:, o:o + wd], q.ap[:, o:o + wd], s, 0.0, ALU.mult, ALU.add, t, tiw,
                                      self.sc_free))
                else:
                    ts.append(self.stt(sc[:, o:o + wd], q.ap[:, o:o + wd], s, sc[:, o:o + wd], ALU.mult, ALU.add, t,
                                       sct[0]))
            q.release(ts)
            sct[0] = ts
        cm = c("cmask", 0, 384)

        def top64():
            t = self.tt(sc, sc, cm, ALU.add, sct[0])
            mx = m["sm"][:, 96:112]
            for r in range(8):
                tn = []
                for o, k, wd in ((0, 0, 128), (128, 8, 256)):
                    s, x = sc[:, o:o + wd], mx[:, k:k + 8]
                    tn.append(self.dve.do(lambda e, s=s, x=x: e.max(x, s), t))
                t2 = []
                for n, (o, k, wd) in enumerate(((0, 0, 128), (128, 8, 256))):
                    s, x = sc[:, o:o + wd], mx[:, k:k + 8]
                    t2.append(self.dve.do(lambda e, s=s, x=x: e.match_replace(s, x, s, PICKED), tn[n]))
                t = t2
            t = self.ts(sc, sc, -3.0e38, NEG, ALU.is_gt, ALU.mult, t)
            return self.tt(sc, sc, cm, ALU.add, t)

        t = self.pair(4, w, l, o_cq, o_cq + 128)
        tcq = ev(CQ.rearrange("p a t -> p (a t)"), 4, t, f0)
        index_head(0)
        index_head(1)
        b = bk[5]
        t = self.unit(b.ap[:, 0:T], cols(w, l, o_ckv), b.free)
        tckv = ev(CKV, 5, t, f0)
        index_head(2)
        index_head(3)
        b = bk[6]
        self.unit(b.ap[0:96, 0:T], cols(w, l, o_kr - 64, 96), b.free, M=96)
        sw = [x for k in range(8) for x in [(w, l, 128 * k, 128, o_kr - 64, 64), (w, l, 128 * k, 128, o_kr + 16, 16),
                                            (w, l, 128 * k, 128, o_kr, 16)]]
        t = self.unit(b.ap[0:96, T:2 * T], sw, M=96)
        q = self.tmp.take()
        rr = slice(64, 96)
        t1 = self.tt(q.ap[rr, 0:T], b.ap[rr, 0:T], m["rope"][rr, 0, :], ALU.mult, t, self.rope_t, q.free)
        t2 = self.tt(q.ap[rr, T:2 * T], b.ap[rr, T:2 * T], m["rope"][rr, 1, :], ALU.mult, t, self.rope_t)
        b.free = [t2]
        t = self.tt(q.ap[rr, 0:T], q.ap[rr, 0:T], q.ap[rr, T:2 * T], ALU.add, t1, t2)
        tkr = self.fn(KM[rr, :, :], q.ap[rr, 0:T].unsqueeze(1).to_broadcast([32, 8, T]), ACT.Identity, t, f2)
        q.release([tkr])
        for h in range(4, 8):
            index_head(h)
        tsel = top64()
        tqa, tka = [], []
        for n, (dst, base, lst) in enumerate(((QA, 0, tqa), (QA, 256, tqa), (KA, 512, tka), (KA, 768, tka))):
            t = self.pair(4 + n, w, l, base, base + 128)
            k = n % 2
            lst.append(ev(dst[:, 2 * k:2 * k + 2, :].rearrange("p a t -> p (a t)"), 4 + n, t, f0))
        t = self.token_major((2, 3), w, l, 1024)
        tva = [ev(VA[:, k, :], 2 + k, t, f1) for k in range(2)]
        tn1 = self.sum_tiles(0, [CQ[:, 0, :], CQ[:, 1, :]], [tcq, tcq], True)
        tn2 = self.sum_tiles(1, [CKV], [tckv], True)
        rep = m["rep"]
        tR1, tv1 = self.inv_sqrt(rep[0][:], rep[1][:], bk[0].ap[:, 0:T], 256, 1e-6, tn1, tmp=rep[2][:])
        bk[0].free = [tv1]
        t1 = self.tt(CQ, CQ, rep[0][:].unsqueeze(1).to_broadcast([128, 2, T]), ALU.mult, tR1, tn1)
        tR2, tv2 = self.inv_sqrt(rep[0][:], rep[1][:], bk[1].ap[:, 0:T], 128, 1e-6, tn2, t1, tR1, tmp=rep[2][:])
        bk[1].free = [tv2]
        t2 = self.tt(CKV, CKV, rep[0][:], ALU.mult, tR2, tn2)
        tga, tgb = [], []
        for n in range(8):
            base, dst, lst = (o_ga, GA, tga) if n < 4 else (o_gb, GB, tgb)
            k = n % 4
            t = self.pair(4 + k, w, l, base + 256 * k, base + 256 * k + 128)
            t = self.fn(dst[:, 2 * k:2 * k + 2, :].rearrange("p a t -> p (a t)"), bk[4 + k].ap, ACT.Sigmoid, t, f3)
            bk[4 + k].free = [t]
            lst.append(t)
        xs_done = (self.pe.sem, self.pe.n)
        YA = [self.XS[:, k, :] for k in range(4)]
        YB = [self.XS[:, 4 + k, :] for k in range(4)]
        HQ = [YB[0], YB[1]]
        HV = YB[2]
        thq = []
        for k, (src, tk, dst, g) in enumerate(((CQ[:, 0, :], t1, YB[0], c(f"q_norm{l}", 0)),
                                               (CQ[:, 1, :], t1, YB[1], c(f"q_norm{l}", 1)),
                                               (CKV, t2, YB[2], c(f"kv_norm{l}")))):
            th = self.fn(dst[:, 0:T], src, ACT.Identity, tk, xs_done, scale=g)
            tl = self.stt(dst[:, T:2 * T], src, g, dst[:, 0:T].bitcast(F32), ALU.mult, ALU.subtract, th, tk)
            thq.append([th, tl])
        tqm = {}
        for hp in range(4):
            blocks = []
            for h in (2 * hp, 2 * hp + 1):
                for swap in range(2):
                    for k in range(2):
                        if not swap:
                            blocks.append(("w_uq_2", l, 128 * k, 128, 96 * h, 96))
                        else:
                            blocks += [("w_uq_2", l, 128 * k, 128, 96 * h, 64), ("w_uq_2", l, 128 * k, 128, 96 * h + 80, 16),
                                       ("w_uq_2", l, 128 * k, 128, 96 * h + 64, 16)]
            W = self.W.take(blocks)
            for n, h in enumerate((2 * hp, 2 * hp + 1)):
                b = bk[4 + h % 2]
                g = []
                for swap in range(2):
                    o = b.ap[0:96, swap * T:swap * T + T]
                    for k in range(2):
                        a = (n * 4 + swap * 2 + k) * 96
                        wh, wl = W[0][:, a:a + 96], W[1][:, a:a + 96]
                        g += [(o, wh, HQ[k][:, 0:T], k == 0, False), (o, wh, HQ[k][:, T:2 * T], False, False),
                              (o, wl, HQ[k][:, 0:T], False, k == 1)]
                tok = self.mms(g, W[2], thq, b.free)
                q = self.tmp.take()
                t1 = self.tt(q.ap[0:96, 0:T], b.ap[0:96, 0:T], m["rope"][0:96, 0, :], ALU.mult, tok, self.rope_t, q.free)
                t2 = self.tt(q.ap[0:96, T:2 * T], b.ap[0:96, T:2 * T], m["rope"][0:96, 1, :], ALU.mult, tok)
                b.free = [t2]
                tqm[h] = self.tt(QM[0:96, h, :], q.ap[0:96, 0:T], q.ap[0:96, T:2 * T], ALU.add, t1, t2, f2)
                q.release([tqm[h]])
            self.W.done(tok)
        tkm = []
        W = self.W.take([("w_ukv_2", l, 0, 128, 128 * h, 128) for h in range(8)])
        for hp in range(4):
            b = bk[6 + hp % 2]
            g = []
            for n in range(2):
                h = 2 * hp + n
                o = b.ap[:, n * T:n * T + T]
                wh, wl = W[0][:, 128 * h:128 * h + 128], W[1][:, 128 * h:128 * h + 128]
                g += [(o, wh, HV[:, 0:T], True, False), (o, wh, HV[:, T:2 * T], False, False),
                      (o, wl, HV[:, 0:T], False, True)]
            tok = self.mms(g, W[2], thq[2], b.free)
            t = self.fn(KM[0:64, 2 * hp:2 * hp + 2, :], b.ap[0:64, :].rearrange("p (a t) -> p a t", a=2), ACT.Identity,
                        tok, f2)
            b.free = [t]
            tkm.append(t)
        self.W.done(tok)
        W = self.W.take([("w_ukv_2", l, 0, 128, 128 * h + 64, 64) for h in range(8)])
        tvm = []
        for tb in range(2):
            b = bk[2 + tb]
            tk, tl = slice(tb * 128, tb * 128 + 128), slice(T + tb * 128, T + tb * 128 + 128)
            tok = self.mms([(b.ap, HV[:, tk], W[0], True, False), (b.ap, HV[:, tl], W[0], False, False),
                            (b.ap, HV[:, tk], W[1], False, True)], W[2], thq[2], b.free)
            t = self.fn(VM[:, tb, :], b.ap, ACT.Identity, tok, f0, sct[0])
            b.free = [t]
            tvm.append(t)
        self.W.done(tok)
        xs_done = (self.pe.sem, self.pe.n)
        tail = {}

        def scores(n):
            h, second = n % 8, n >= 8
            b = bk[4 + n % 2]
            if not second:
                r = slice(64 * (h % 2), 64 * (h % 2) + 64)
                t = self.mms([(b.ap[:, 0:128], QA[r, h // 2, 0:128], KA[r, h // 2, 0:128], True, True),
                              (b.ap[:, 128:384], QA[r, h // 2, 128:256], KA[r, h // 2, :], True, True)],
                             tqa, tka, b.free)
            else:
                r = slice(0, 96)
                t = self.mms([(b.ap[:, 0:128], QM[r, h, 0:128], KM[r, h, 0:128], True, True),
                              (b.ap[:, 128:384], QM[r, h, 128:256], KM[r, h, :], True, True)],
                             tqm[h], tkm, tkr, b.free)
            q = self.tmp.take()
            s = q.ap[:, 0:384]
            if not second:
                t = self.stt(s, b.ap[:, 0:384], 0.125, self.Bz[:, h, :], ALU.mult, ALU.add, t, self.bias_t, q.free)
                b.free = [t]
                t = self.tt(s, s, sc, ALU.add, t, tsel)
            else:
                t = self.stt(s, b.ap[:, 0:384], 96.0 ** -0.5, cm, ALU.mult, ALU.add, t, q.free)
                b.free = [t]
            st = self.stat(n)
            t1 = self.red(st[:, 0:1], s[:, 0:128], t)
            t2 = self.red(st[:, 1:2], s[:, 128:384], t)
            t3 = self.ts(st[:, 2:4], st[:, 0:2], -1.0, None, ALU.mult, None, t1, t2)
            tail[n], tb = self.exps(n, s[:, 0:128], s[:, 128:384], st, 1.0, t3)
            q.release([tb])

        def value(n):
            h, second = n % 8, n >= 8
            vv = VM if second else VA
            t = self.turn(n, tail[n])
            v = [vv[:, k, 64 * h:64 * h + 64] for k in range(2)]
            part = slice(64 * (h % 2), 64 * (h % 2) + 64)
            t, _ = self.pv(n, v[0], v[1], t, tvm if second else tva, part, first=h % 2 == 0)
            if h % 2:
                dst = (YB if second else YA)[h // 2]
                b = bk[7]
                th = self.fn(dst[:, 0:T], b.ap[:, 0:T], ACT.Identity, t, xs_done)
                tl = self.tt(dst[:, T:2 * T], b.ap[:, 0:T], dst[:, 0:T].bitcast(F32), ALU.subtract, th)
                b.free = [tl]
                ys[n // 2] = [th, tl]

        ys = {}
        for n in range(18):
            if n < 16:
                scores(n)
            if n >= 2:
                value(n - 2)
        self.sc_free = [tsel]
        outs = {}

        def emit_out(k):
            o, wt = outs[k]
            tok = self.out_k(k, 8, "w_out_2", l, o.ap[:, 0:T], o.ap[:, T:2 * T], wt)
            o.release([tok])
            return tok

        for n in range(8):
            W = self.W.take([("w_branch_a_2", l, 128 * k, 128, 128 * n, 128) for k in range(4)]
                            + [("w_branch_b_2", l, 128 * k, 128, 128 * n, 128) for k in range(4)])
            b = bk[4 + n % 4]
            g = []
            for s, Y in enumerate((YA, YB)):
                for k in range(4):
                    a = (4 * s + k) * 128
                    wh, wl = W[0][:, a:a + 128], W[1][:, a:a + 128]
                    o = b.ap[:, s * T:s * T + T]
                    g += [(o, wh, Y[k][:, 0:T], k == 0, False), (o, wh, Y[k][:, T:2 * T], False, False),
                          (o, wl, Y[k][:, 0:T], False, k == 3)]
            tok = self.mms(g, W[2], [ys[k] for k in range(8)], b.free)
            self.W.done(tok)
            q = self.tmp.take()
            t1 = self.tt(q.ap[:, 0:T], b.ap[:, 0:T], GA[:, n, :], ALU.mult, tok, tga, q.free)
            t2 = self.tt(q.ap[:, T:2 * T], b.ap[:, T:2 * T], GB[:, n, :], ALU.mult, tok, tgb)
            b.free = [t2]
            t = self.tt(q.ap[:, 0:T], q.ap[:, 0:T], q.ap[:, T:2 * T], ALU.add, t1, t2)
            outs[n] = self.split_out(q.ap[:, 0:T], t)
            q.release(outs[n][1])
            if n >= 1:
                emit_out(n - 1)
        self.xs_free = [(self.pe.sem, self.pe.n)]
        tok = emit_out(7)
        fin = [tok, t2]
        self.bfree = [fin, fin, fin, fin]
        self.post_norm(l, 0, tok)

    def ffn(self, l):
        m, c = self.m, self.c
        self.modulate(l, 1)
        outs = {}

        def emit_out(k):
            o, wt = outs[k]
            tok = self.out_k(k, 22, "w_down_2", l, o.ap[:, 0:T], o.ap[:, T:2 * T], wt)
            o.release([tok])
            return tok

        for i in range(0, 22, 2):
            acc = []
            for v in range(2):
                bank = (4 if i % 4 == 0 else 6) + v
                b = self.bank[bank]
                t = self.pair(bank, "w_up_2", l, (22 * v + i) * 128, (22 * v + i + 1) * 128)
                a = self.tmp.take()
                ta = []
                for k in range(2):
                    ch = 22 * v + i + k
                    ta.append(self.fn(a.ap[:, k * T:k * T + T], b.ap[:, k * T:k * T + T], ACT.Identity, t, a.free,
                                      scale=c(f"conv_w{l}", 88 + ch), bias=c(f"conv_b{l}", ch)))
                both = list(ta)
                for s in (1, 2):
                    for k in range(2):
                        ch = 22 * v + i + k
                        o = a.ap[:, k * T + s:k * T + T]
                        ta[k] = self.stt(o, b.ap[:, k * T:k * T + T - s], c(f"conv_w{l}", (2 - s) * 44 + ch), o,
                                         ALU.mult, ALU.add, both, ta[k])
                b.free = [ta[1]]
                acc.append((a, ta))
                if i >= 2:
                    emit_out(i - 2 + v)
            (g, tg), (v, tv) = acc
            t = self.fn(g.ap, g.ap, ACT.Silu, tg)
            t = self.tt(g.ap, g.ap, v.ap, ALU.mult, t, tv)
            v.release([t])
            for k in range(2):
                outs[i + k] = self.split_out(g.ap[:, k * T:k * T + T], t)
            g.release(outs[i][1] + outs[i + 1][1])
        self.xs_free = [(self.pe.sem, self.pe.n)]
        emit_out(20)
        tok = emit_out(21)
        self.post_norm(l, 1, tok)

    def run(self):
        m = self.m
        self.ada_i, self.mod_t, self.sc_free = 0, [[], []], []
        s = self.s
        sp = self.sp
        self.tconst = sp.dma(lambda e: e.dma_start(m["C"][:], self.cst), s["const"], 16)
        tx = sp.dma(lambda e: e.dma_start(m["X"][:], self.xin), s["x"], 16)
        self.tpos = sp.dma(lambda e: e.dma_start(m["pos"][:], self.posr), s["pos"], 16)
        for e in (self.pe, self.act, self.dve):
            e.wait(self.tconst, tx)
        self.W = Weights(self, self.known)
        self.xt = [tx] * 8
        self.silu_t = self.fn(m["silu_c"][:], self.c("c", 0, 8), ACT.Silu)
        self.make_rope()
        self.layer_a(0)
        self.layer_b()
        self.make_bias()
        self.layer_c()
        self.some_background(len(self.background))
        self.layer_a(1)
        self.ada(96)
        for l in range(2):
            self.mixer(l)
            self.ffn(l)
        n = self.ndbg if self.dbg is not None else 0
        t = sp.dma(lambda e: e.dma_start(self.out, m["X"][:]), s["out"], 16 * (n + 1), self.xt)
        sp.wait(t)


def constants(inp):
    C = np.zeros((128, NCONST), np.float32)

    def put(name, a):
        o, n = COFF[name]
        a = np.asarray(a)
        C[0:a.shape[0], o:o + n] = a

    def vec(a):
        return np.asarray(a).reshape(-1, 128).T

    for j in range(2):
        put(f"a_norm{j}", vec(inp["a_norm"][j]))
        put(f"a_conv_w{j}", vec(inp["a_conv_w"][j]))
        for n in ("a_conv_b", "a_ln_g", "a_ln_b"):
            put(f"{n}{j}", vec(inp[n][j]))
    for n in ("b_norm", "b_q_norm", "b_k_norm", "c_norm", "c_conv_w"):
        put(n, vec(inp[n][0]))
    put("b_f_bias", np.asarray(inp["b_f_bias"][0]).reshape(16, 1))
    for l in range(2):
        put(f"b_ada{l}", vec(inp["b_ada_2"][l]))
        put(f"conv_w{l}", vec(inp["conv_w_2"][l]))
        put(f"conv_b{l}", vec(inp["conv_b_2"][l]))
        for n in ("ln1_g", "ln1_b", "ln2_g", "ln2_b"):
            put(f"{n}{l}", vec(inp[n + "_2"][l]))
        put(f"q_norm{l}", vec(inp["q_norm_g_2"][l]))
        put(f"kv_norm{l}", vec(inp["kv_norm_g_2"][l]))
    put("c", vec(inp["c_2"][0]))
    put("rel_bias", np.broadcast_to(np.asarray(inp["rel_bias_2"]).reshape(1, 256), (128, 256)))
    put("ident", np.eye(128, dtype=np.float32))
    tri = np.where(np.arange(128)[None, :] <= np.arange(128)[:, None], 0.0, NEG).astype(np.float32)
    put("cmask", np.concatenate([tri, np.zeros((128, 128), np.float32), tri], axis=1))
    hot = np.zeros((128, 31), np.float32)
    hot[:, 15] = 1.0
    put("onehot", hot)
    put("ones", np.ones((128, 128), np.float32))
    freq = np.float32(10000.0) ** (-np.arange(16, dtype=np.float32) * np.float32(2.0 / 32))
    col = np.zeros((128, 1), np.float32)
    col[64:80, 0] = col[80:96, 0] = freq
    put("freq", col)
    mul = np.zeros((128, 2), np.float32)
    mul[64:80, 0], mul[80:96, 0] = -1.0, 1.0
    put("ropemul", mul)
    return C


def stream(pieces, inp):
    W = np.empty((128, sum(wd for _, wd in pieces)), np.float32)
    at = 0
    for blocks, _ in pieces:
        for name, layer, r0, nr, c0, n in blocks:
            W[:, at:at + n] = inp[name][layer, r0:r0 + nr, c0:c0 + n]
            at += n
    return W


def lay(nc, arrays, dbg=None):
    pos = np.asarray(arrays["positions_2"], np.int32).reshape(T)
    posr = np.empty((128, T + 2), np.int32)
    posr[:, 0:T] = pos[None, :]
    posr[:, T:T + 2] = pos.reshape(2, 128).T
    x = np.ascontiguousarray(np.asarray(arrays["x"])[0].T.reshape(8, 128, T).transpose(1, 0, 2))
    cst = constants(arrays)
    ins = {"in_cst": cst, "in_pos": posr, "in_x": x}
    aps = {k: nc.dram_tensor(k, v.shape, mybir.dt.from_np(v.dtype), kind="ExternalInput").ap() for k, v in ins.items()}
    out = nc.dram_tensor("out_x", (128, 8, T), F32, kind="ExternalOutput").ap()

    def w_stream_of(width):
        return nc.dram_tensor("in_w", (128, width), F32, kind="ExternalInput").ap()

    pieces = build(nc, w_stream_of, aps["in_cst"], aps["in_pos"], aps["in_x"], out, dbg)
    ins["in_w"] = stream(pieces, arrays)
    return ins


def kernel(**inputs):
    import concourse.bacc as _bacc
    from concourse.bass_utils import run_bass_kernel_spmd as _run

    nc = _bacc.Bacc("TRN2", target_bir_lowering=False, num_devices=1)
    arrays = {k: np.asarray(v) for k, v in inputs.items()}
    ins = lay(nc, arrays)
    r = _run(nc, [ins], core_ids=[0])
    y = r.results[0]["out_x"]
    return np.ascontiguousarray(y.transpose(1, 0, 2).reshape(D, T).T).reshape(1, T, D)
```

```python
import math
from contextlib import ExitStack

import numpy as np

import concourse.bass as bass
from concourse import mybir

F32 = mybir.dt.float32
F32R = mybir.dt.float32r
I32 = mybir.dt.int32
ALU = mybir.AluOpType
ACT = mybir.ActivationFunctionType
AX = mybir.AxisListType.X

T = 256
D = 1024
E = 2048
NEG = -1.0e30
PICKED = -3.4e38
ALPHA = 4.0 ** 0.25
PIECE = 1024
NRAW = 8
NHL = 4
LOOK = 3
MAGIC = 12582912.0
POOL_TAPS = 11
TWO_PI = [6.28125, 0.0019350051879882812, 3.019916050561733e-07]

CONSTS = (
    [(f"a_norm{j}", 8) for j in range(2)]
    + [(f"a_conv_w{j}", 31 * 16) for j in range(2)]
    + [(f"{n}{j}", 16) for n in ("a_conv_b", "a_ln_g", "a_ln_b") for j in range(2)]
    + [("b_norm", 8), ("b_q_norm", 1), ("b_k_norm", 1), ("b_f_bias", 1), ("c_norm", 8), ("c_conv_w", 48)]
    + [(f"b_ada{l}", 48) for l in range(2)]
    + [(f"conv_w{l}", 132) for l in range(2)]
    + [(f"conv_b{l}", 44) for l in range(2)]
    + [(f"{n}{l}", 8) for n in ("ln1_g", "ln1_b", "ln2_g", "ln2_b") for l in range(2)]
    + [(f"q_norm{l}", 2) for l in range(2)]
    + [(f"kv_norm{l}", 1) for l in range(2)]
    + [("rel_bias", 256), ("ident", 128), ("cmask", 384), ("onehot", 31), ("ones", 128), ("freq", 1),
       ("ropemul", 2)]
)
COFF = {}
_at = 0
for _name, _n in CONSTS:
    COFF[_name] = (_at, _n)
    _at += _n
NCONST = _at


def bucket_starts():
    n = np.arange(0, 129).astype(np.float32)
    ratio = np.log(np.maximum(n, 1) / np.float32(16)) / np.float32(math.log(128 / 16))
    large = np.minimum(16 + (ratio * np.float32(16)).astype(np.int32), 31)
    large = np.where(n < 16, 0, large)
    return [int(np.argmax(large >= b)) for b in range(16, 32)]


class Eng:

    def __init__(self, sem):
        self.sem, self.n, self.q, self.seen = sem, 0, [], {}

    def wait(self, *toks):
        for t in toks:
            if t is None:
                continue
            if isinstance(t, list):
                self.wait(*t)
                continue
            sem, val = t
            if self.seen.get(sem.name, 0) < val:
                self.seen[sem.name] = val
                self.q.append((0, sem, val))

    def do(self, f, *toks):
        self.wait(*toks)
        self.n += 1
        self.q.append((1, f, self.sem, 1))
        return (self.sem, self.n)

    def quiet(self, f, *toks):
        self.wait(*toks)
        self.q.append((1, f, None, 0))

    def dma(self, f, sem, count, *toks):
        self.wait(*toks)
        self.q.append((1, f, sem, 16))
        return (sem, count)

    def play(self, e):
        for item in self.q:
            if item[0] == 0:
                e.wait_ge(item[1], item[2])
            else:
                ins = item[1](e)
                if item[2] is not None:
                    ins.then_inc(item[2], item[3])


class Buf:

    def __init__(self, ap):
        self.ap, self.free, self.held = ap, [], False

    def release(self, toks):
        self.free, self.held = toks, False


class Ring:

    def __init__(self, aps):
        self.b, self.i = [Buf(a) for a in aps], 0

    def take(self):
        for _ in self.b:
            b = self.b[self.i % len(self.b)]
            self.i += 1
            if not b.held:
                b.held = True
                return b
        raise RuntimeError("every buffer of the ring is held")


def build(nc, w_stream_of, cst, posr, cbr, xin, out, dbg=None):
    with ExitStack() as ctx:
        def sb(name, shape, dt=F32):
            return ctx.enter_context(nc.sbuf_tensor(name, shape, dt))

        mem = dict(
            C=sb("C", [128, NCONST]),
            X=sb("X", [128, 8, T]),
            XS=sb("XS", [128, 8, 2 * T], F32R),
            YS=sb("YS", [128, 4, 2 * T], F32R),
            B=[sb(f"B{i}", [128, 4096]) for i in range(4)],
            raw=[sb(f"raw{i}", [128, PIECE]) for i in range(NRAW)],
            wh=[sb(f"wh{i}", [128, PIECE], F32R) for i in range(NHL)],
            wl=[sb(f"wl{i}", [128, PIECE], F32R) for i in range(NHL)],
            os=[sb(f"os{i}", [128, 2 * T], F32R) for i in range(4)],
            t=[sb(f"tmp{i}", [128, 512]) for i in range(6)],
            rep=[sb(f"rep{i}", [128, T]) for i in range(4)],
            rope=sb("rope", [128, 2, T]),
            mod=sb("mod", [128, 2, 48]),
            sm=sb("sm", [128, 128]),
            cb=sb("cb", [128, D]),
            sc=sb("sc", [128, 384]),
            fold=sb("fold", [128, 32]),
            pos=sb("pos", [128, T + 2], I32),
            ps=[ctx.enter_context(nc.psum_tensor(f"ps{i}", [128, 512], F32)) for i in range(8)],
        )
        sems = {n: ctx.enter_context(nc.semaphore("s_" + n)) for n in
                ["pe", "act", "dve", "pool", "sp", "const", "x", "pos", "cb", "out"] + [f"raw{i}" for i in range(NRAW)]}
        plan = Program(nc, mem, sems, None, cst, posr, cbr, xin, out, dbg)
        plan.run()
        pieces = plan.W.pieces
        width = sum(wd for _, wd, _ in pieces)
        prog = Program(nc, mem, sems, pieces, cst, posr, cbr, xin, out, dbg)
        prog.wdram = w_stream_of(width)
        prog.run()
        block = ctx.enter_context(nc.Block())
        block.sync(prog.sp.play)
        block.scalar(prog.act.play)
        block.vector(prog.dve.play)
        block.gpsimd(prog.pool.play)
        block.tensor(prog.pe.play)
    return [(blocks, wd) for blocks, wd, _ in pieces]


class Weights:

    def __init__(self, p, pieces):
        self.p, self.known, self.pieces, self.i = p, pieces, [], 0
        self.split = {}
        self.used = {}
        self.late = []
        if pieces is not None:
            self.off = np.cumsum([0] + [wd for _, wd, _ in pieces]).tolist()
            self.loaded = {}
            for i in range(NRAW):
                self.load(i, [])
            for i in range(LOOK):
                self.make(i)

    def load(self, i, toks):
        if i >= len(self.known):
            return
        p, a, b, s = self.p, self.off[i], self.off[i + 1], i % NRAW
        self.loaded[i] = p.sp.dma(lambda e: e.dma_start(p.m["raw"][s][:, 0:b - a], p.wdram[:, a:b]),
                                  p.s[f"raw{s}"], 16 * (i // NRAW + 1), toks)

    def raw(self, i):
        return self.p.m["raw"][i % NRAW][:, 0:self.known[i][1]]

    def make(self, i):
        if i >= len(self.known) or self.known[i][2]:
            return
        p, wd, s = self.p, self.known[i][1], i % NHL
        raw, hi, lo = self.raw(i), p.m["wh"][s][:, 0:wd], p.m["wl"][s][:, 0:wd]
        free = self.used.get(s)
        th = p.act.do(lambda e: e.copy(hi, raw), self.loaded[i], free)
        tl = p.dve.do(lambda e: e.tensor_tensor(lo, raw, hi.bitcast(F32), ALU.subtract), self.loaded[i], th, free)
        self.split[i] = [th, tl]
        self.load(i + NRAW, [th, tl])

    def take(self, blocks, plain=False):
        i = self.i
        self.i += 1
        wd = sum(b[5] for b in blocks)
        self.pieces.append((blocks, wd, plain))
        if self.known is None:
            m = self.p.m
            return m["wh"][0][:, 0:wd] if not plain else m["raw"][0][:, 0:wd], m["wl"][0][:, 0:wd], []
        if plain:
            return self.raw(i), None, [self.loaded[i]]
        while i not in self.split:
            self.make(self.late.pop(0))
        s = i % NHL
        return self.p.m["wh"][s][:, 0:wd], self.p.m["wl"][s][:, 0:wd], self.split[i]

    def done(self, tok, split=True):
        i = self.i - 1
        if self.known is None:
            return
        if not self.known[i][2]:
            self.used[i % NHL] = tok
        if self.known[i][2]:
            self.load(i + NRAW, [tok])
        self.late.append(i + LOOK)
        if split:
            while self.late:
                self.make(self.late.pop(0))


def cols(name, layer, c0, n=128, kt=8):
    return [(name, layer, 128 * k, 128, c0, n) for k in range(kt)]


class Program:
    def __init__(self, nc, mem, sems, pieces, cst, posr, cbr, xin, out, dbg):
        self.nc, self.m, self.s = nc, mem, sems
        self.cst, self.posr, self.cbr, self.xin, self.out, self.dbg = cst, posr, cbr, xin, out, dbg
        self.pe, self.act, self.dve, self.pool, self.sp = (Eng(sems[n]) for n in ("pe", "act", "dve", "pool", "sp"))
        self.wdram = None
        self.known = pieces
        self.bank = [Buf(b[:]) for b in mem["ps"]]
        self.tmp = Ring([t[:] for t in mem["t"]])
        self.osr = Ring([t[:] for t in mem["os"]])
        self.X = mem["X"]
        self.XS = mem["XS"]
        self.xt = [None] * 8
        self.xs_t = [None] * 8
        self.xs_free = []
        self.bfree = [[] for _ in range(4)]
        self.background = []
        self.ndbg = 0

    def c(self, name, k=0, n=1, rows=slice(0, 128)):
        o = COFF[name][0] + k
        return self.m["C"][rows, o:o + n]

    def tt(self, o, a, b, op, *w, eng=None):
        return (eng or self.dve).do(lambda e: e.tensor_tensor(o, a, b, op), *w)

    def ts(self, o, a, s1, s2, op0, op1, *w, eng=None):
        if op1 is None:
            return (eng or self.dve).do(lambda e: e.tensor_scalar(o, a, s1, None, op0), *w)
        return (eng or self.dve).do(lambda e: e.tensor_scalar(o, a, s1, s2, op0, op1), *w)

    def stt(self, o, a, s, b, op0, op1, *w, eng=None):
        return (eng or self.dve).do(lambda e: e.scalar_tensor_tensor(out=o, in0=a, scalar=s, in1=b, op0=op0, op1=op1), *w)

    def cp(self, o, a, *w):
        return self.dve.do(lambda e: e.tensor_copy(o, a), *w)

    def fn(self, o, a, f, *w, **kw):
        return self.act.do(lambda e: e.activation(o, a, f, **kw), *w)

    def mms(self, group, *w, skip=False, last=True):
        self.pe.wait(*w)
        for n, (o, a, b, st, sp) in enumerate(group):
            f = (lambda e, o=o, a=a, b=b, st=st, sp=sp: e.matmul(o, a, b, start=st, stop=sp, skip_group_check=skip)
                 if skip else e.matmul(o, a, b, start=st, stop=sp))
            if last and n == len(group) - 1:
                return self.pe.do(f)
            self.pe.quiet(f)

    def some_background(self, budget=None):
        while self.background and (budget is None or budget > 0):
            cost, job = self.background.pop(0)
            job()
            if budget is not None:
                budget -= cost

    def xh(self, k):
        return self.XS[:, k, 0:T]

    def xl(self, k):
        return self.XS[:, k, T:2 * T]

    def split_pairs(self, kt, hi, lo, W, M):
        g = []
        for k in range(kt):
            wh, wl = W[0][:, k * M:(k + 1) * M], W[1][:, k * M:(k + 1) * M]
            g += [(wh, hi(k)), (wh, lo(k)), (wl, hi(k))]
        return g

    def unit(self, out, blocks, *w, M=128, kt=8):
        W = self.W.take(blocks)
        self.pe.wait(W[2], *w)
        for k in range(kt):
            wh, wl = W[0][:, k * M:(k + 1) * M], W[1][:, k * M:(k + 1) * M]
            tok = self.mms([(out, wh, self.xh(k), k == 0, False), (out, wh, self.xl(k), False, False),
                            (out, wl, self.xh(k), False, k == kt - 1)], self.xs_t[k], last=k == kt - 1)
        self.W.done(tok)
        return tok

    def plain_unit(self, out, blocks, X, xt, *w):
        W = self.W.take(blocks, plain=True)
        self.pe.wait(W[2], *w)
        for k in range(8):
            tok = self.mms([(out, W[0][:, k * 128:(k + 1) * 128], X[:, k, :], k == 0, k == 7)], xt[k], last=k == 7)
        self.W.done(tok)
        return tok

    def plain_pair(self, bank, name, layer, c0, X, xt, between):
        b = self.bank[bank]
        self.plain_unit(b.ap[:, 0:T], cols(name, layer, c0), X, xt, b.free)
        between()
        tok = self.plain_unit(b.ap[:, T:2 * T], cols(name, layer, c0 + 128), X, xt)
        between()
        return tok

    def pair(self, bank, name, layer, c0, c1, *w, between=None):
        b = self.bank[bank]
        self.unit(b.ap[:, 0:T], cols(name, layer, c0), b.free, *w)
        if between:
            between()
        tok = self.unit(b.ap[:, T:2 * T], cols(name, layer, c1))
        if between:
            between()
        return tok

    def token_major(self, banks, name, layer, c0, n=512, colmap=None):
        for kp in range(4):
            blocks = []
            for k in (2 * kp, 2 * kp + 1):
                if colmap is None:
                    blocks.append((name, layer, 128 * k, 128, c0, n))
                else:
                    blocks += [(name, layer, 128 * k, 128, a, m) for a, m in colmap]
            W = self.W.take(blocks)
            for tb in range(2):
                tk = slice(tb * 128, tb * 128 + 128)
                tl = slice(T + tb * 128, T + tb * 128 + 128)
                o = self.bank[banks[tb]].ap[:, 0:n]
                g = []
                for kk in range(2):
                    k = 2 * kp + kk
                    wh, wl = W[0][:, kk * n:(kk + 1) * n], W[1][:, kk * n:(kk + 1) * n]
                    g += [(self.XS[:, k, tk], wh), (self.XS[:, k, tl], wh), (self.XS[:, k, tk], wl)]
                tok = self.mms([(o, a, b, kp == 0 and i == 0, kp == 3 and i == 5) for i, (a, b) in enumerate(g)],
                               W[2], self.xs_t, self.bank[banks[tb]].free if kp == 0 else None, skip=True)
            self.W.done(tok)
        return tok

    def split_out(self, src, *w):
        o = self.osr.take()
        th = self.act.do(lambda e: e.copy(o.ap[:, 0:T], src), *w, o.free)
        tl = self.tt(o.ap[:, T:2 * T], src, o.ap[:, 0:T].bitcast(F32), ALU.subtract, *w, th)
        return o, [th, tl]

    def out_k(self, k, K, name, layer, hi, lo, *w):
        W = self.W.take([(name, layer, 128 * k, 128, 0, D)])
        g = []
        for m in range(8):
            o = self.bank[m // 2].ap[:, (m % 2) * T:(m % 2) * T + T]
            wh, wl = W[0][:, m * 128:(m + 1) * 128], W[1][:, m * 128:(m + 1) * 128]
            g += [(o, wh, hi, k == 0 and m % 2 == 0, False), (o, wh, lo, False, False),
                  (o, wl, hi, False, k == K - 1)]
        self.pe.wait(W[2], *w, [self.bank[i].free for i in range(4)] if k == 0 else None)
        if k < K - 1:
            tok = self.mms(g, skip=True)
        else:
            self.sums_t = [self.mms(g[6 * i:6 * i + 6], skip=True) for i in range(4)]
            tok = self.sums_t[3]
        self.W.done(tok)
        return tok

    def residual(self):
        for i in range(4):
            o = self.X[:, 2 * i:2 * i + 2, :]
            s = self.bank[i].ap.rearrange("p (a t) -> p a t", a=2)
            t = self.tt(o, o, s, ALU.add, self.sums_t[i], self.xt)
            self.bank[i].free = [t]
            self.xt[2 * i] = self.xt[2 * i + 1] = t
        self.dump()

    def dump(self):
        if self.dbg is not None:
            k = self.ndbg
            t = self.sp.dma(lambda e: e.dma_start(self.dbg[k], self.X[:]), self.s["out"], 16 * (k + 1), self.xt)
            self.xt = [[x, t] for x in self.xt]
        self.ndbg += 1

    def inv_sqrt(self, o, v, src, n, eps, *w, tmp):
        t = self.ts(v, src, 1.0 / n, eps, ALU.mult, ALU.add, *w)
        return self.root(o, v, tmp, t), t

    def root(self, o, v, tmp, *w):
        t = self.fn(tmp, v, ACT.Sqrt, *w)
        t = self.dve.do(lambda e: e.reciprocal(o, tmp), t)
        t = self.tt(tmp, o, o, ALU.mult, t)
        t = self.stt(tmp, tmp, -0.5, v, ALU.mult, ALU.mult, t)
        return self.stt(o, tmp, 1.5, o, ALU.add, ALU.mult, t)

    def table(self, f):
        self.act.quiet(lambda e: e.preload_act_table(f))

    def square(self, src, *w):
        q = self.tmp.take()
        return q, self.fn(q.ap[:, 0:T], src, ACT.Square, *w, q.free)

    def token_sum(self, bank, col, tile, start, stop, *w):
        o = self.bank[bank].ap
        return self.mms([(o[:, col + b:col + b + 1], tile[:, 128 * b:128 * b + 128], self.c("ones", 0, 1),
                          start and b == 0, stop) for b in range(2)], *w, skip=True)

    def spread(self, bank, src, *w):
        b = self.bank[bank]
        n = src.shape[1]
        return self.mms([(b.ap[:, 128 * k:128 * k + 128], src[:, k:k + 1].to_broadcast([128, 128]),
                          self.c("ident", 0, 128), True, True) for k in range(n)], *w, b.free)

    def mean_root(self, sums, spread, n, eps, tok):
        st = self.m["sm"][:, 112:128]
        b = self.bank[sums]
        mu, R, v, s, d = st[:, 0:2], st[:, 2:4], st[:, 4:6], st[:, 6:8], st[:, 8:10]
        t1 = self.ts(mu, b.ap[:, 0:2], 1.0 / n, None, ALU.mult, None, tok, self.sm_free)
        t2 = self.ts(v, b.ap[:, 2:4], 1.0 / n, eps, ALU.mult, ALU.add, tok)
        b.free = [t2]
        t3 = self.tt(s, mu, mu, ALU.mult, t1)
        t4 = self.tt(v, v, s, ALU.subtract, t3, t2)
        tr = self.root(R, v, d, t4)
        t = self.spread(spread, st[:, 0:4], tr, t1)
        self.sm_free = [t]
        return self.bank[spread].ap[:, 0:T], self.bank[spread].ap[:, T:2 * T], t

    def rms_in(self, gname, plain=False):
        xn = self.m["B"][3][:, 0:2048].rearrange("p (a t) -> p a t", a=8)
        st = self.m["sm"][:, 112:128]
        self.table(ACT.Sqrt)
        for m in range(8):
            q, tq = self.square(self.X[:, m, :], self.xt[m])
            tok = self.token_sum(6, 0, q.ap, m == 0, m == 7, tq, self.bank[6].free)
            q.release([tok])
        t, tv = self.inv_sqrt(st[:, 0:2], st[:, 2:4], self.bank[6].ap[:, 0:2], D, 1e-6, tok, self.sm_free,
                              tmp=st[:, 4:6])
        self.bank[6].free = [tv]
        t = self.spread(7, st[:, 0:2], t)
        self.sm_free = [t]
        R = self.bank[7].ap[:, 0:T]
        toks, hi = [], {}

        def low(m):
            tl = self.tt(self.xl(m), xn[:, m, :], self.xh(m).bitcast(F32), ALU.subtract, hi[m])
            self.xs_t[m] = [hi[m], tl]

        for m in range(8):
            g = self.c(gname, m)
            t1 = self.stt(xn[:, m, :], self.X[:, m, :], g, R, ALU.mult, ALU.mult, t, self.bfree[3])
            toks.append([t1])
            self.bank[7].free = [t1]
            if not plain:
                hi[m] = self.act.do(lambda e, m=m: e.copy(self.xh(m), xn[:, m, :]), t1, self.xs_free)
                if m >= 1:
                    low(m - 1)
        if plain:
            for m in range(8):
                hi[m] = self.act.do(lambda e, m=m: e.copy(self.xh(m), xn[:, m, :]), toks[m], self.xs_free)
            for m in range(8):
                low(m)
        else:
            low(7)
            self.bfree[3] = [self.xs_t[7]]
        return xn, toks

    def layer_a(self, j):
        m, c = self.m, self.c
        XG, xgt = self.rms_in(f"a_norm{j}", plain=True)
        if j == 0:
            self.act.wait(self.tconst)
            self.silu_t = self.fn(m["cb"][:], m["cb"][:], ACT.Silu, self.tcb)
            self.make_rope()
        U = m["B"][3][:, 2048:4096].rearrange("p (i t) -> p i t", i=8)
        A = m["B"][1][:].rearrange("p (i t) -> p i t", i=16)
        Z = m["B"][0][:].rearrange("p (i t) -> p i t", i=16)
        ut, at, sq, tz, conv_done = {}, {}, {}, [], {}
        w_conv, b_conv = f"a_conv_w{j}", f"a_conv_b{j}"

        acc = {}

        def conv_start(p):
            b = self.bank[p % 2]
            for n in range(2):
                i = 2 * p + n
                u, o = U[:, i % 8, :], b.ap[:, n * T:n * T + T]
                self.fn(o[:, 0:1], c(b_conv, i), ACT.Identity, b.free)
                t = self.fn(o[:, 1:T], u[:, 0:T - 1], ACT.Identity, ut[p], scale=c(w_conv, 29 * 16 + i),
                            bias=c(b_conv, i))
            acc[2 * p] = acc[2 * p + 1] = t
            for i in (2 * p, 2 * p + 1):
                at[i] = self.fn(A[:, i, :], U[:, i % 8, :], ACT.Identity, self.bfree[1], scale=c(w_conv, 30 * 16 + i))

        def conv_step(p, k):
            s = 30 - k
            q = self.tmp.take() if k < POOL_TAPS else None
            done = []
            for i in (2 * p, 2 * p + 1):
                u, w, h = U[:, i % 8, 0:T - s], c(w_conv, k * 16 + i), (i % 2) * T
                if q is None:
                    o = self.bank[p % 2].ap[:, h + s:h + T]
                    acc[i] = self.stt(o, u, w, o, ALU.mult, ALU.add, ut[p], acc[i])
                else:
                    x = q.ap[:, h + s:h + T]
                    t = self.fn(x, u, ACT.Identity, ut[p], q.free, scale=w)
                    at[i] = self.tt(A[:, i, s:T], A[:, i, s:T], x, ALU.add, t, at[i], eng=self.pool)
                    done.append(at[i])
            if q is not None:
                q.release(done)

        def conv_end(p):
            i, b = 2 * p, self.bank[p % 2]
            o = A[:, i:i + 2, :].rearrange("p a t -> p (a t)")
            conv_done[p] = [at[i], at[i + 1]]
            at[i] = at[i + 1] = self.tt(o, b.ap, o, ALU.add, acc[i], acc[i + 1], at[i], at[i + 1])
            b.free = [at[i]]

        def stats(i):
            q, tq = self.square(A[:, i, :], at[i])
            self.token_sum(2, 0, A[:, i, :], i == 0, i == 15, at[i], self.bank[2].free)
            sq[i] = self.token_sum(2, 2, q.ap, False, i == 15, tq)
            q.release([sq[i]])

        def gates(p):
            b = self.bank[4 + nb[0] % 4]
            nb[0] += 1
            t = self.pair(4 + (nb[0] - 1) % 4, "a_w_in", j, 2 * E + p * 256, 2 * E + p * 256 + 128, between=work)
            t = self.fn(Z[:, 2 * p:2 * p + 2, :].rearrange("p a t -> p (a t)"), b.ap, ACT.Silu, t, self.bfree[0])
            b.free = [t]
            tz.append(t)

        a, b = list(range(28, POOL_TAPS - 1, -1)), list(range(POOL_TAPS - 1, -1, -1))
        order = [k for _, k in sorted([((n + 0.5) / len(a), k) for n, k in enumerate(a)] +
                                      [((n + 0.5) / len(b), k) for n, k in enumerate(b)])]
        todo = []

        def work(n=6):
            for _ in range(min(n, len(todo))):
                todo.pop(0)()

        nb = [0]
        for p in range(9):
            if p < 8:
                ng, nv = 4 + nb[0] % 4, 4 + (nb[0] + 1) % 4
                nb[0] += 2
                tg = self.plain_pair(ng, "a_w_in", j, E + p * 256, XG, xgt, work)
                sg = self.tmp.take()
                t1 = self.fn(sg.ap, self.bank[ng].ap, ACT.Sigmoid, tg, sg.free)
                self.bank[ng].free = [t1]
                if p % 2 == 0:
                    tv = self.plain_pair(nv, "a_w_in", j, p * 256, XG, xgt, work)
                else:
                    tv = self.pair(nv, "a_w_in", j, p * 256, p * 256 + 128, between=work)
            if p == 8:
                gates(6)
                gates(7)
                work(len(todo))
            elif p >= 1:
                work(len(todo))
            if p < 8:
                a = 2 * p % 8
                ut[p] = self.tt(U[:, a:a + 2, :].rearrange("p a t -> p (a t)"), self.bank[nv].ap, sg.ap, ALU.mult,
                                tv, t1, self.bfree[3], conv_done.get(p - 4))
                self.bank[nv].free = [ut[p]]
                sg.release([ut[p]])
            if p >= 1:
                conv_end(p - 1)
            if p < 8:
                todo += [lambda p=p: conv_start(p)] + [lambda p=p, k=k: conv_step(p, k) for k in order]
            if p >= 2:
                stats(2 * p - 4)
                stats(2 * p - 3)
                if p < 8:
                    gates(p - 2)
        xg_done = self.xs_free = [self.pe_now()]
        stats(14)
        stats(15)
        self.table(ACT.Sqrt)
        mu, R, tr = self.mean_root(2, 7, E, 1e-6, sq[15])
        self.table(ACT.Silu)
        y, outs = {}, {}
        for i in range(0, 22, 2):
            if i < 16:
                a = A[:, i:i + 2, :]
                bc = mu.unsqueeze(1).to_broadcast([128, 2, T])
                t = self.tt(a, a, bc, ALU.subtract, at[i], at[i + 1], sq[i], sq[i + 1], tr)
                t = self.tt(a, a, R.unsqueeze(1).to_broadcast([128, 2, T]), ALU.mult, t)
                self.bank[7].free = [t]
                y[i] = [self.fn(A[:, k, :], A[:, k, :], ACT.Silu, t, scale=c(f"a_ln_g{j}", k),
                                bias=c(f"a_ln_b{j}", k)) for k in (i, i + 1)]
            if 2 <= i < 18:
                a = A[:, i - 2:i, :]
                tm = self.tt(a, a, Z[:, i - 2:i, :], ALU.mult, y[i - 2], tz[i // 2 - 1])
                for k in (i - 2, i - 1):
                    outs[k] = self.split_out(A[:, k, :], tm)
            for k in (i - 4, i - 3):
                if 0 <= k < 16:
                    o, w = outs[k]
                    tok = self.out_k(k, 16, "a_w_out", j, o.ap[:, 0:T], o.ap[:, T:2 * T], w)
                    o.release([tok])
        self.bfree[3] = [tr, xg_done]
        self.bfree[1] = [w[0], w[1]]
        self.bfree[0] = [tm]
        self.residual()

    def layer_b(self):
        m, c = self.m, self.c
        self.rms_in("b_norm")
        K = m["B"][0][:].rearrange("p (i t) -> p i t", i=16)
        Q = m["B"][1][:].rearrange("p (i t) -> p i t", i=16)
        V = m["B"][3][:].rearrange("p (b e) -> p b e", b=2)
        I16 = c("ident", 0, 16, rows=slice(0, 16))
        b = self.bank[4]
        tf = self.unit(b.ap[:, 0:T], cols("b_w_in", 0, 4 * E - 112), b.free)
        tb = self.tmp.take()
        f = tb.ap[:, 0:T]
        t = self.fn(f, b.ap[:, 0:T], ACT.Identity, tf, tb.free)
        b.free = [t]
        b6 = self.bank[6]
        t = self.mms([(b6.ap[0:16, 0:T], c("ident", 112, 16), f, True, True)], t, b6.free)
        tb.release([t])
        y, e1, lf, cc, ncs = (self.m["rep"][1][0:16, :], self.m["rep"][2][0:16, :], self.m["rep"][3][0:16, :],
                              self.m["B"][2][0:16, 3840:4096], self.m["rep"][0][0:16, :])
        t = self.ts(y, b6.ap[0:16, 0:T], c("b_f_bias", 0, 1, rows=slice(0, 16)), None, ALU.add, None, t)
        b6.free = [t]
        ta = self.fn(e1, y, ACT.Abs, t)
        ta = self.fn(e1, e1, ACT.Exp, ta, scale=-1.0)
        ta = self.fn(e1, e1, ACT.Ln, ta, bias=1.0)
        t = self.stt(lf, y, 0.0, e1, ALU.min, ALU.subtract, t, ta)
        t = self.dve.do(lambda e: e.tensor_tensor_scan(out=cc, data0=self.c("ones", 0, 128, rows=slice(0, 16))[:, 0:1]
                                                       .to_broadcast([16, T]), data1=lf, initial=0.0,
                                                       op0=ALU.mult, op1=ALU.add), t)
        tn = self.ts(ncs, cc, -1.0, None, ALU.mult, None, t)
        ct = m["sm"][:, 0:32]
        g = [(b6.ap[:, 16 * k:16 * k + 16], cc[:, 128 * k:128 * k + 128], I16, True, True) for k in range(2)]
        tp = self.mms(g, t, b6.free)
        tct = self.cp(ct, b6.ap[:, 0:32], tp)
        b6.free = [tct]
        tv = []
        for n in range(4):
            banks = (4, 5) if n % 2 == 0 else (6, 7)
            tok = self.token_major(banks, "b_w_in", 0, 2 * E + 512 * n)
            for k in range(2):
                bb = self.bank[banks[k]]
                o = V[:, k, 512 * n:512 * n + 512]
                t = self.fn(o, bb.ap, ACT.Identity, tok, self.bfree[3]) if k else self.cp(o, bb.ap, tok, self.bfree[3])
                bb.free = [t]
                tv.append(t)
            self.some_background(8)
        rows = {}

        def squares(ss, last):
            if last is None:
                return
            q, t2, i = last
            for h in (i, i + 1):
                t = self.mms([(ss.ap[0:16, 0:T], c("onehot", 15 - h, 16), q.ap[:, (h - i) * T:(h - i) * T + T],
                               h == 0, h == 15)], t2, ss.free if h == 0 else None)
            q.release([t])

        for which, (dst, base, sbank, bf) in enumerate(((K, E, 0, 0), (Q, 0, 1, 1))):
            kt, last = [], None
            ss = self.bank[sbank]
            for n, i in enumerate(range(0, 16, 2)):
                bb = self.bank[4 + n % 4]
                t = self.pair(4 + n % 4, "b_w_in", 0, base + i * 128, base + i * 128 + 128)
                q = self.tmp.take()
                t1 = self.fn(dst[:, i:i + 2, :].rearrange("p a t -> p (a t)"), bb.ap, ACT.Identity, t, self.bfree[bf])
                t2 = self.fn(q.ap, bb.ap, ACT.Square, t, q.free)
                bb.free = [t1, t2]
                kt.append(t1)
                squares(ss, last)
                last = (q, t2, i)
                self.some_background(8)
            squares(ss, last)
            ts = self.pe_now()
            sq_tmp = self.tmp.take()
            r = m["rep"][3 - which][0:16, :]
            v, s = m["rep"][1][0:16, :], sq_tmp.ap[0:16, 0:T]
            t, tv_ = self.inv_sqrt(r, v, ss.ap[0:16, 0:T], 128, 1e-6, ts, sq_tmp.free, tmp=s)
            ss.free = [tv_]
            sq_tmp.release([t])
            if which:
                t = self.ts(r, r, 128.0 ** -0.5, None, ALU.mult, None, t)
            rows[which] = (r, t, kt)
        ctr = ct.rearrange("p (b h) -> p b h", b=2)
        ready, tail, ex = {}, {}, {}

        def scale_qk(h):
            b = self.bank[4]
            sel = I16[:, h:h + 1].to_broadcast([16, 128])
            t = self.mms([(b.ap[:, 0:T], sel, rows[0][0], True, True), (b.ap[:, T:2 * T], sel, rows[1][0], True, True)],
                         rows[0][1], rows[1][1], b.free)
            t1 = self.stt(K[:, h, :], K[:, h, :], c("b_k_norm"), b.ap[:, 0:T], ALU.mult, ALU.mult, t, rows[0][2][h // 2])
            t2 = self.stt(Q[:, h, :], Q[:, h, :], c("b_q_norm"), b.ap[:, T:2 * T], ALU.mult, ALU.mult, t,
                          rows[1][2][h // 2])
            b.free = [t2]
            ready[h] = [t1, t2]

        def scores(h):
            b = self.bank[5]
            sel = I16[:, h:h + 1].to_broadcast([16, 128])
            idn, tri = c("ident", 0, 128), c("cmask", 0, 128)
            o0, o1, o1d = b.ap[:, 0:128], b.ap[:, 128:384], b.ap[:, 256:384]
            t = self.mms([(o0, Q[:, h, 0:128], K[:, h, 0:128], True, False), (o0, sel, ncs[:, 0:128], False, False),
                          (o0, idn, tri, False, True),
                          (o1, Q[:, h, 128:256], K[:, h, :], True, False), (o1, sel, ncs, False, False),
                          (o1d, idn, tri, False, True)], ready[h], tn, b.free)
            st = self.stat(h)
            t1 = self.red(st[:, 0:1], o0, t)
            t2 = self.red(st[:, 1:2], o1, t)
            t3 = self.tt(st[:, 2:4], st[:, 0:2], ctr[:, :, h], ALU.add, t1, t2, tct)
            t4 = self.tt(st[:, 2:4], ctr[:, :, h], st[:, 2:4], ALU.subtract, t3)
            pt = self.exps(h, o0, o1, st, 1.0, t4)
            b.free = [pt[1]]
            ex[h] = pt[0]

        def value(h):
            t = self.pv(V[:, 0, h * 128:h * 128 + 128], V[:, 1, h * 128:h * 128 + 128], turned[h], tv, slice(0, 128),
                        first=False, bank=6 + h % 2)
            b, q = self.bank[6 + h % 2], self.tmp.take()
            th = self.fn(q.ap[:, T:2 * T], b.ap[:, T:2 * T], ACT.Tanh, t, q.free, scale=0.5)
            tz = self.stt(q.ap[:, T:2 * T], q.ap[:, T:2 * T], 1.0, b.ap[:, T:2 * T], ALU.add, ALU.mult, th)
            t = self.stt(q.ap[:, 0:T], b.ap[:, 0:T], 0.5, q.ap[:, T:2 * T], ALU.mult, ALU.mult, tz)
            b.free = [t]
            o, w = self.split_out(q.ap[:, 0:T], t)
            q.release(w)
            outs[h] = (o, w)

        outs, turned = {}, {}
        for s in range(16 + 3):
            if s < 16:
                scale_qk(s)
            if 0 <= s - 1 < 16:
                scores(s - 1)
                self.some_background(3)
                tail[s - 1] = self.norm(ex[s - 1])
            if 0 <= s - 2 < 16:
                b = self.bank[6 + s % 2]
                self.unit(b.ap[:, T:2 * T], cols("b_w_in", 0, 3 * E + (s - 2) * 128), b.free)
                turned[s - 2] = self.turn(tail[s - 2], 7 - s % 2)
            self.some_background(3)
            if s >= 3:
                h = s - 3
                o, w = outs[h]
                tok = self.out_k(h, 16, "b_w_out", 0, o.ap[:, 0:T], o.ap[:, T:2 * T], w)
                o.release([tok])
            if 0 <= s - 2 < 16:
                value(s - 2)
        self.xs_free = [self.pe_now()]
        fin = [tok, w[1]]
        self.bfree[0] = self.bfree[1] = self.bfree[3] = fin
        self.residual()

    def stat(self, h):
        k = 32 + 8 * (h % 4)
        return self.m["sm"][:, k:k + 8]

    def red(self, o, a, *w):
        return self.dve.do(lambda e: e.tensor_reduce(o, a, AX, ALU.max), *w)

    def exps(self, h, s0, s1, st, scale, *w):
        P = self.tmp.take()
        ta = self.fn(P.ap[:, 0:128], s0, ACT.Exp, *w, P.free, bias=st[:, 2:3], scale=scale, accum_out=st[:, 4:5])
        tb = self.fn(P.ap[:, 128:384], s1, ACT.Exp, *w, bias=st[:, 3:4], scale=scale, accum_out=st[:, 5:6])
        return (P, st, [ta, tb]), tb

    def norm(self, e):
        P, st, t = e
        t = self.dve.do(lambda e: e.reciprocal(st[:, 6:8], st[:, 4:6]), t)
        t1 = self.ts(P.ap[:, 0:128], P.ap[:, 0:128], st[:, 6:7], None, ALU.mult, None, t)
        t2 = self.ts(P.ap[:, 128:384], P.ap[:, 128:384], st[:, 7:8], None, ALU.mult, None, t)
        return P, [t1, t2]

    def turn(self, tail, bank=6):
        P, w = tail
        b = self.bank[bank]
        idn = self.c("ident", 0, 128)
        self.pe.wait(w, b.free)
        for k in range(3):
            a, o = P.ap[:, 128 * k:128 * k + 128], b.ap[:, 128 * k:128 * k + 128]
            f = lambda e, a=a, o=o: e.transpose(o, a, idn)
            if k < 2:
                self.pe.quiet(f)
            else:
                t = self.pe.do(f)
        t = self.fn(P.ap[:, 0:384], b.ap[:, 0:384], ACT.Identity, t)
        b.free = [t]
        return P, t

    def pv(self, v0, v1, turned, tv, part, first=True, bank=7):
        b, (P, t) = self.bank[bank], turned
        t = self.mms([(b.ap[part, 0:T], v0, P.ap[:, 0:T], True, False),
                      (b.ap[part, 128:T], v1, P.ap[:, 256:384], False, True)], t, tv, b.free if first else None)
        P.release([t])
        return t

    def pe_now(self):
        return (self.pe.sem, self.pe.n)

    def layer_c(self):
        m, c = self.m, self.c
        self.rms_in("c_norm")
        outs = {}

        def emit_out(k):
            o, w = outs[k]
            tok = self.out_k(k, 16, "c_w_out", 0, o.ap[:, 0:T], o.ap[:, T:2 * T], w)
            o.release([tok])
            return tok

        for i in range(0, 16, 2):
            tk = self.pair(4, "c_w_in", 0, 2 * E + i * 128, 2 * E + i * 128 + 128)
            cs = self.tmp.take()
            t = self.fn(cs.ap, self.bank[4].ap, ACT.Identity, tk, cs.free)
            self.bank[4].free = [t]
            self.some_background(5)
            tk = self.pair(5, "c_w_in", 0, i * 128, i * 128 + 128)
            tcu = self.tt(cs.ap, self.bank[5].ap, cs.ap, ALU.mult, tk, t)
            self.bank[5].free = [tcu]
            self.some_background(5)
            ac = self.tmp.take()
            tk = self.pair(6, "c_w_in", 0, E + i * 128, E + i * 128 + 128)
            ta = []
            for k in range(2):
                a, u = ac.ap[:, k * T:k * T + T], cs.ap[:, k * T:k * T + T]
                ta.append(self.fn(a, u, ACT.Identity, tcu, ac.free, scale=c("c_conv_w", 32 + i + k)))
            for s in (1, 2):
                for k in range(2):
                    a, u = ac.ap[:, k * T + s:k * T + T], cs.ap[:, k * T:k * T + T - s]
                    ta[k] = self.stt(a, u, c("c_conv_w", (2 - s) * 16 + i + k), a, ALU.mult, ALU.add, ta[k])
            t = self.tt(ac.ap, self.bank[6].ap, ac.ap, ALU.mult, tk, ta)
            self.bank[6].free = [t]
            cs.release([t])
            if i >= 2:
                emit_out(i - 2)
            self.some_background(5)
            tk = self.pair(7, "c_w_in", 0, 3 * E + i * 128, 3 * E + i * 128 + 128)
            if i >= 2:
                emit_out(i - 1)
            zs = self.tmp.take()
            tz = self.fn(zs.ap, self.bank[7].ap, ACT.Silu, tk, zs.free)
            self.bank[7].free = [tz]
            t = self.tt(ac.ap, ac.ap, zs.ap, ALU.mult, t, tz)
            zs.release([t])
            for k in range(2):
                outs[i + k] = self.split_out(ac.ap[:, k * T:k * T + T], t)
            ac.release(outs[i][1] + outs[i + 1][1])
            self.some_background(5)
        self.xs_free = [self.pe_now()]
        emit_out(14)
        tok = emit_out(15)
        self.residual()

    def ada(self, l):
        md = self.m["mod"][:, l, :]

        def job(u):
            W = self.W.take([("w_ada_2", l, 128 * u, 128, 0, D, True)], plain=True)
            t = self.dve.do(lambda e: e.scalar_tensor_tensor(out=W[0], in0=W[0], scalar=1.0, in1=self.m["cb"][:],
                                                             op0=ALU.mult, op1=ALU.mult, accum_out=md[:, u:u + 1]),
                            W[2], self.silu_t)
            self.W.done(t, split=False)

        def finish(n):
            o = md[:, 8 * n:8 * n + 8]
            t = self.tt(o, o, self.c(f"b_ada{l}", 8 * n, 8), ALU.add, (self.dve.sem, self.dve.n))
            if n in (1, 4):
                t = self.ts(o, o, 1.0, None, ALU.add, None, t)
            self.mod_t[l].append(t)
        jobs = []
        for n in range(6):
            jobs += [(3, lambda u=u: job(u)) for u in range(8 * n, 8 * n + 8)] + [(1, lambda n=n: finish(n))]
        return jobs

    def need_mod(self, l, n):
        while len(self.mod_t[l]) < n:
            self.background.pop(0)[1]()

    def later(self, jobs):
        a, b = self.background, jobs
        order = sorted([(i / max(1, len(a)), 0, i) for i in range(len(a))] +
                       [(i / max(1, len(b)), 1, i) for i in range(len(b))])
        self.background = [(a, b)[w][i] for _, w, i in order]

    def enter_high(self, k, tok, scale, shift):
        q = self.tmp.take()
        t = self.fn(q.ap[:, 0:T], self.X[:, k, :], ACT.Identity, tok, q.free,
                    scale=scale[:, k:k + 1], bias=shift[:, k:k + 1])
        return k, q, self.act.do(lambda e: e.copy(self.xh(k), q.ap[:, 0:T]), t, self.xs_free)

    def enter_low(self, k, q, th):
        tl = self.tt(self.xl(k), q.ap[:, 0:T], self.xh(k).bitcast(F32), ALU.subtract, th, self.xs_free)
        q.release([tl, th])
        self.xs_t[k] = [th, tl]

    def first_modulate(self):
        md = self.m["mod"][:, 0, :]
        self.act.wait(self.mod_t[0])
        last = None
        for k in range(8):
            now = self.enter_high(k, self.xt[k], md[:, 8:16], md[:, 0:8])
            if last:
                self.enter_low(*last)
            last = now
        self.enter_low(*last)
        for k in range(8):
            self.xt[k] = self.ts(self.X[:, k, :], self.X[:, k, :], ALPHA, None, ALU.mult, None, self.xs_t[k])

    def post_norm(self, l, which, tok):
        self.need_mod(l, 5 if which == 0 else 6)
        if (l, which) == (0, 1):
            self.need_mod(1, 2)
        md = self.m["mod"][:, l, :]
        g = 16 if which == 0 else 40
        n = "ln1" if which == 0 else "ln2"
        lng, lnb = self.c(f"{n}_g{l}", 0, 8), self.c(f"{n}_b{l}", 0, 8)
        final = (l, which) == (1, 1)
        self.table(ACT.Sqrt)
        for k in range(8):
            x = self.X[:, k, :]
            b = self.bank[k // 2]
            t = self.stt(x, b.ap[:, (k % 2) * T:(k % 2) * T + T], md[:, g + k:g + k + 1], x, ALU.mult, ALU.add,
                         self.sums_t[k // 2], self.xt[k], self.mod_t[l])
            b.free = [t]
            self.xt[k] = t
            q, tq = self.square(x, t)
            self.token_sum(6, 0, x, k == 0, k == 7, t, self.bank[6].free)
            ts = self.token_sum(6, 2, q.ap, False, k == 7, tq)
            q.release([ts])
        fold = self.m["fold"]
        gs, bs, ga, ba = (fold[:, 8 * i:8 * i + 8] for i in range(4))
        if not final:
            l2, o = (l, 24) if which == 0 else (l + 1, 0)
            md2 = self.m["mod"][:, l2, :]
            t5 = self.tt(gs, lng, md2[:, o + 8:o + 16], ALU.mult, self.mod_t[l2])
            t6 = self.tt(bs, lnb, md2[:, o + 8:o + 16], ALU.mult, self.mod_t[l2])
            t6 = self.tt(bs, bs, md2[:, o:o + 8], ALU.add, t6)
            t7 = self.ts(ga, lng, ALPHA, None, ALU.mult, None)
            t8 = self.ts(ba, lnb, ALPHA, None, ALU.mult, None)
        mu, R, tr = self.mean_root(6, 7, D, 1e-5, ts)
        if not final:
            self.act.wait(t5, t6)
        nt, last = [], []
        for i in range(4):
            a = self.X[:, 2 * i:2 * i + 2, :]
            u = self.tt(a, a, mu.unsqueeze(1).to_broadcast([128, 2, T]), ALU.subtract, tr, self.xt)
            u = self.tt(a, a, R.unsqueeze(1).to_broadcast([128, 2, T]), ALU.mult, u)
            nt += [u, u]
            self.bank[7].free = [u]
            if not final:
                now = [self.enter_high(k, u, gs, bs) for k in (2 * i, 2 * i + 1)]
                for x in last:
                    self.enter_low(*x)
                last = now
        for x in last:
            self.enter_low(*x)
        if final:
            for k in range(8):
                self.xt[k] = self.fn(self.X[:, k, :], self.X[:, k, :], ACT.Identity, nt[k],
                                     scale=lng[:, k:k + 1], bias=lnb[:, k:k + 1])
        else:
            for k in range(8):
                self.xt[k] = self.fn(self.X[:, k, :], self.X[:, k, :], ACT.Identity, nt[k], t7, t8,
                                     scale=ga[:, k:k + 1], bias=ba[:, k:k + 1])
        self.dump()

    def make_bias(self):
        m, c = self.m, self.c
        Bz = m["B"][2][:, 0:8 * 384].rearrange("p (h s) -> p h s", h=8)
        n, bk = m["B"][2][:, 3072:3456], m["B"][2][:, 3456:3840]
        eq = [m["sc"][:], n]
        st = {}
        back = []

        def start():
            q = self.tmp.take()
            pf = q.ap[:, 0:T + 2]
            t = self.cp(pf, m["pos"][:], self.tpos, q.free)
            for o, k, w in ((0, 0, 128), (128, 1, 256)):
                st["n%d" % k] = self.ts(n[:, o:o + w], pf[:, 0:w], pf[:, T + k:T + k + 1], -1.0, ALU.subtract,
                                        ALU.mult, t)
            q.release([st["n0"], st["n1"]])
            t = self.ts(n, n, 0.0, None, ALU.max, None, st["n0"], st["n1"])
            st["n"] = t
            st["b"] = self.ts(bk, n, 15.0, None, ALU.min, None, t)
        back.append((1, start))
        for thr in bucket_starts():
            def step(thr=thr):
                st["b"] = self.stt(bk, n, float(thr), bk, ALU.is_ge, ALU.add, st["n"], st["b"])
            back.append((1, step))
        for b in range(32):
            def mask(b=b):
                st["m", b] = self.ts(eq[b % 2], bk, float(b), None, ALU.is_equal, None, st["b"], st.get(("u", b - 2)))
            back.append((1, mask))
            for h in range(8):
                def add(b=b, h=h):
                    r = c("rel_bias", b * 8 + h)
                    if b == 0:
                        t = self.ts(Bz[:, h, :], eq[0], r, None, ALU.mult, None, st["m", 0])
                    else:
                        t = self.stt(Bz[:, h, :], eq[b % 2], r, Bz[:, h, :], ALU.mult, ALU.add, st["m", b],
                                     st["h", h])
                    st["h", h] = t
                    st["u", b] = t
                back.append((1, add))

        def finish():
            self.bias_t = [st["h", h] for h in range(8)]
        back.append((1, finish))
        self.Bz = Bz
        return back

    def make_rope(self):
        m, c = self.m, self.c
        r = slice(64, 96)
        C, S = m["rope"][:, 0, :], m["rope"][:, 1, :]
        q, q2 = self.tmp.take(), self.tmp.take()
        a, k, w, pf = q.ap[r, 0:T], q.ap[r, T:2 * T], q2.ap[r, 0:T], q2.ap[r, T:2 * T]
        t0 = self.dve.do(lambda e: e.memset(m["rope"][0:64, 0, :], 1.0))
        t00 = self.dve.do(lambda e: e.memset(m["rope"][0:64, 1, :], 0.0))
        t = self.cp(pf, m["pos"][r, 0:T], self.tpos, q2.free, q.free)
        t = self.ts(a, pf, c("freq", 0, 1, rows=r), None, ALU.mult, None, t, self.tconst)
        t = self.ts(k, a, 1.0 / (2 * math.pi), MAGIC, ALU.mult, ALU.add, t)
        t = self.ts(k, k, -MAGIC, None, ALU.add, None, t)
        for part in TWO_PI:
            t = self.stt(a, k, -part, a, ALU.mult, ALU.add, t)
        t = self.ts(a, a, 3.1415925, -3.1415925, ALU.min, ALU.max, t)
        ts = self.fn(S[r, :], a, ACT.Sin, t)
        t = self.ts(w, a, -1.0, None, ALU.mult, None, t)
        t = self.tt(w, w, a, ALU.max, t)
        t = self.ts(w, w, -1.0, math.pi / 2, ALU.mult, ALU.add, t)
        tc = self.fn(C[r, :], w, ACT.Sin, t)
        t = self.ts(S[r, :], S[r, :], c("ropemul", 0, 1, rows=r), None, ALU.mult, None, ts)
        q.release([tc, ts, t])
        q2.release([tc, ts, t])
        self.rope_t = [t0, t00, t, tc]

    def mixer(self, l):
        m, c = self.m, self.c
        w = "w_in_2"
        o_iq, o_ik, o_iw, o_cq, o_ckv, o_kr, o_ga, o_gb = 1536, 2048, 2112, 2120, 2376, 2504, 2536, 3560
        B0 = m["B"][1]
        QA = B0[:, 0:1024].rearrange("p (i t) -> p i t", i=4)
        KA = B0[:, 1024:2048].rearrange("p (i t) -> p i t", i=4)
        IQ = B0[:, 2048:3072].rearrange("p (i t) -> p i t", i=4)
        VM = B0[:, 2048:3072].rearrange("p (b e) -> p b e", b=2)
        IK = B0[:, 3072:3328]
        CQ = B0[:, 3328:3840].rearrange("p (i t) -> p i t", i=2)
        CKV = B0[:, 3840:4096]
        GA = m["B"][3][:, 0:2048].rearrange("p (i t) -> p i t", i=8)
        GB = m["B"][3][:, 2048:4096].rearrange("p (i t) -> p i t", i=8)
        QM = m["B"][0][:, 0:2048].rearrange("p (i t) -> p i t", i=8)
        KM = m["B"][0][:, 2048:4096].rearrange("p (i t) -> p i t", i=8)
        VA = m["B"][2][:, 3072:4096].rearrange("p (b e) -> p b e", b=2)
        f0, f1, f2, f3 = self.bfree[1], self.bfree[2], self.bfree[0], self.bfree[3]
        bk = self.bank

        def ev(o, bank, *w, eng="a"):
            b = bk[bank]
            t = self.fn(o, b.ap[:, 0:o_size(o)], ACT.Identity, *w) if eng == "a" else self.cp(o, b.ap[:, 0:o_size(o)], *w)
            b.free = [t]
            return t

        def o_size(o):
            return o.shape[1] if len(o.shape) == 2 else o.shape[1] * o.shape[2]

        b = bk[6]
        self.unit(b.ap[0:96, 0:T], [x for k in range(8) for x in [(w, l, 128 * k, 128, o_iw, 64),
                                                                  (w, l, 128 * k, 128, o_kr, 32)]], b.free, M=96)
        sw = [x for k in range(8) for x in [(w, l, 128 * k, 128, o_kr - 64, 64), (w, l, 128 * k, 128, o_kr + 16, 16),
                                            (w, l, 128 * k, 128, o_kr, 16)]]
        t = self.unit(b.ap[0:96, T:2 * T], sw, M=96)
        qw = self.tmp.take()
        tw = self.ts(qw.ap[0:8, 0:T], b.ap[0:8, 0:T], 8.0 ** -0.5, None, ALU.mult, None, t, qw.free)
        q = self.tmp.take()
        rr = slice(64, 96)
        t1 = self.tt(q.ap[rr, 0:T], b.ap[rr, 0:T], m["rope"][rr, 0, :], ALU.mult, t, self.rope_t, q.free)
        t2 = self.tt(q.ap[rr, T:2 * T], b.ap[rr, T:2 * T], m["rope"][rr, 1, :], ALU.mult, t, self.rope_t)
        b.free = [t2]
        t = self.tt(q.ap[rr, 0:T], q.ap[rr, 0:T], q.ap[rr, T:2 * T], ALU.add, t1, t2)
        tkr = self.fn(KM[rr, :, :], q.ap[rr, 0:T].unsqueeze(1).to_broadcast([32, 8, T]), ACT.Identity, t, f2)
        q.release([tkr])
        b = bk[5]
        t = self.unit(b.ap[:, 0:T], [x for k in range(8) for x in [(w, l, 128 * k, 128, o_ik, 64)] * 2], b.free)
        tik = ev(IK, 5, t, f0)
        b = bk[4]
        t = self.mms([(b.ap[:, 8 * k:8 * k + 8], qw.ap[0:8, 128 * k:128 * k + 128], c("ident", 0, 8, rows=slice(0, 8)),
                       True, True) for k in range(2)], tw, b.free)
        qw.release([t])
        iw = m["sm"][:, 64:80]
        tiw = self.cp(iw, b.ap[:, 0:16], t)
        b.free = [tiw]
        tiq = []
        for n in range(2):
            t = self.pair(6 + n, w, l, o_iq + 256 * n, o_iq + 256 * n + 128)
            tiq.append(ev(IQ[:, 2 * n:2 * n + 2, :].rearrange("p a t -> p (a t)"), 6 + n, t, f0))
        sc = m["sc"][:]
        sct = [None]

        def index_head(h):
            b = bk[2 + h % 2]
            r = slice(64 * (h % 2), 64 * (h % 2) + 64)
            t = self.mms([(b.ap[:, 0:128], IQ[r, h // 2, 0:128], IK[r, 0:128], True, True),
                          (b.ap[:, 128:384], IQ[r, h // 2, 128:256], IK[r, :], True, True)], tik, tiq, b.free)
            q = self.tmp.take()
            t = self.fn(q.ap[:, 0:384], b.ap[:, 0:384], ACT.Relu, t, q.free, scale=0.125)
            b.free = [t]
            ts = []
            for o, k, wd in ((0, 0, 128), (128, 1, 256)):
                s = iw[:, 8 * k + h:8 * k + h + 1]
                if h == 0:
                    ts.append(self.ts(sc[:, o:o + wd], q.ap[:, o:o + wd], s, 0.0, ALU.mult, ALU.add, t, tiw,
                                      self.sc_free))
                else:
                    ts.append(self.stt(sc[:, o:o + wd], q.ap[:, o:o + wd], s, sc[:, o:o + wd], ALU.mult, ALU.add, t,
                                       sct[0]))
            q.release(ts)
            sct[0] = ts
        cm = c("cmask", 0, 384)

        top = {}

        def top64():
            mx = m["sm"][:, 96:112]
            halves = ((0, 0, 128), (128, 8, 256))

            def start():
                top["t"] = self.tt(sc, sc, cm, ALU.add, sct[0])

            def find(n):
                o, k, wd = halves[n]
                s, x = sc[:, o:o + wd], mx[:, k:k + 8]
                t = self.dve.do(lambda e: e.max(x, s), top["t"], top.get(n))
                top[n] = self.dve.do(lambda e: e.match_replace(s, x, s, PICKED), t)

            def finish():
                t = self.ts(sc, sc, -3.0e38, NEG, ALU.is_gt, ALU.mult, top[0], top[1])
                top["sel"] = self.tt(sc, sc, cm, ALU.add, t)
            self.background = [(1, start)] + [(2, lambda n=n: find(n)) for _ in range(8) for n in (0, 1)] + [(2, finish)] + \
                self.background

        t = self.pair(4, w, l, o_cq, o_cq + 128)
        tcq = ev(CQ.rearrange("p a t -> p (a t)"), 4, t, f0)
        index_head(0)
        index_head(1)
        b = bk[5]
        t = self.unit(b.ap[:, 0:T], cols(w, l, o_ckv), b.free)
        tckv = ev(CKV, 5, t, f0)
        index_head(2)
        index_head(3)
        for h in range(4, 8):
            index_head(h)
        top64()
        tqa, tka = [], []
        for n, (dst, base, lst) in enumerate(((QA, 0, tqa), (QA, 256, tqa), (KA, 512, tka), (KA, 768, tka))):
            t = self.pair(4 + n, w, l, base, base + 128)
            k = n % 2
            lst.append(ev(dst[:, 2 * k:2 * k + 2, :].rearrange("p a t -> p (a t)"), 4 + n, t, f0))
            if n == 0:
                self.table(ACT.Sqrt)
                for i, (src, tk) in enumerate(((CQ[:, 0, :], tcq), (CQ[:, 1, :], tcq), (CKV, tckv))):
                    q, tq = self.square(src, tk)
                    tn = self.token_sum(0, 2 * (i // 2), q.ap, i == 0, i > 0, tq, bk[0].free)
                    q.release([tn])
                self.table(ACT.Tanh)
            if n == 1:
                st = m["sm"][:, 112:128]
                ta = self.ts(st[:, 0:2], bk[0].ap[:, 0:2], 1.0 / 256, 1e-6, ALU.mult, ALU.add, tn, self.sm_free)
                tb = self.ts(st[:, 2:4], bk[0].ap[:, 2:4], 1.0 / 128, 1e-6, ALU.mult, ALU.add, tn)
                bk[0].free = [tb]
                tr = self.root(st[:, 4:8], st[:, 0:4], st[:, 8:12], ta, tb)
                tr = self.spread(1, st[:, 4:8], tr)
                self.sm_free = [tr]
                t1 = self.tt(CQ, CQ, bk[1].ap[:, 0:T].unsqueeze(1).to_broadcast([128, 2, T]), ALU.mult, tr)
                t2 = self.tt(CKV, CKV, bk[1].ap[:, T:2 * T], ALU.mult, tr)
                bk[1].free = [t2]
            if n != 0:
                self.some_background(3)
        YA = [m["YS"][:, k, :] for k in range(4)]
        YB_ = [self.osr.take() for _ in range(4)]
        YB = [o.ap for o in YB_]
        HQ, HV = [YA[0], YA[1]], YA[2]
        thq = []
        for k, (src, tk, g) in enumerate(((CQ[:, 0, :], t1, c(f"q_norm{l}", 0)), (CQ[:, 1, :], t1, c(f"q_norm{l}", 1)),
                                          (CKV, t2, c(f"kv_norm{l}")))):
            dst = YA[k]
            th = self.fn(dst[:, 0:T], src, ACT.Identity, tk, self.ys_free, scale=g)
            tl = self.stt(dst[:, T:2 * T], src, g, dst[:, 0:T].bitcast(F32), ALU.mult, ALU.subtract, th, tk)
            thq.append([th, tl])
        t = self.token_major((2, 3), w, l, 1024)
        tva = [ev(VA[:, k, :], 2 + k, t, f1) for k in range(2)]
        tga, tgb = {}, {}
        self.some_background(8)
        tqm = {}
        for hp in range(4):
            blocks = []
            for h in (2 * hp, 2 * hp + 1):
                for swap in range(2):
                    for k in range(2):
                        if not swap:
                            blocks.append(("w_uq_2", l, 128 * k, 128, 96 * h, 96))
                        else:
                            blocks += [("w_uq_2", l, 128 * k, 128, 96 * h, 64),
                                       ("w_uq_2", l, 128 * k, 128, 96 * h + 80, 16),
                                       ("w_uq_2", l, 128 * k, 128, 96 * h + 64, 16)]
            W = self.W.take(blocks)
            for n, h in enumerate((2 * hp, 2 * hp + 1)):
                b = bk[4 + h % 4]
                g = []
                for swap in range(2):
                    o = b.ap[0:96, swap * T:swap * T + T]
                    for k in range(2):
                        a = (n * 4 + swap * 2 + k) * 96
                        wh, wl = W[0][:, a:a + 96], W[1][:, a:a + 96]
                        g += [(o, wh, HQ[k][:, 0:T], k == 0, False), (o, wh, HQ[k][:, T:2 * T], False, False),
                              (o, wl, HQ[k][:, 0:T], False, k == 1)]
                tok = self.mms(g, W[2], thq, b.free)
                q = self.tmp.take()
                t1 = self.tt(q.ap[0:96, 0:T], b.ap[0:96, 0:T], m["rope"][0:96, 0, :], ALU.mult, tok, self.rope_t,
                             q.free)
                t2 = self.tt(q.ap[0:96, T:2 * T], b.ap[0:96, T:2 * T], m["rope"][0:96, 1, :], ALU.mult, tok)
                b.free = [t2]
                tqm[h] = self.tt(QM[0:96, h, :], q.ap[0:96, 0:T], q.ap[0:96, T:2 * T], ALU.add, t1, t2, f2)
                q.release([tqm[h]])
            self.W.done(tok)
        tkm = []
        W = self.W.take([("w_ukv_2", l, 0, 128, 128 * h, 128) for h in range(8)])
        for hp in range(4):
            b = bk[hp % 2]
            g = []
            for n in range(2):
                h = 2 * hp + n
                o = b.ap[:, n * T:n * T + T]
                wh, wl = W[0][:, 128 * h:128 * h + 128], W[1][:, 128 * h:128 * h + 128]
                g += [(o, wh, HV[:, 0:T], True, False), (o, wh, HV[:, T:2 * T], False, False),
                      (o, wl, HV[:, 0:T], False, True)]
            tok = self.mms(g, W[2], thq[2], b.free)
            t = self.fn(KM[0:64, 2 * hp:2 * hp + 2, :], b.ap[0:64, :].rearrange("p (a t) -> p a t", a=2), ACT.Identity,
                        tok, f2)
            b.free = [t]
            tkm.append(t)
        self.W.done(tok)
        W = self.W.take([("w_ukv_2", l, 0, 128, 128 * h + 64, 64) for h in range(8)])
        tvm = []
        for tb in range(2):
            b = bk[2 + tb]
            tk, tl = slice(tb * 128, tb * 128 + 128), slice(T + tb * 128, T + tb * 128 + 128)
            tok = self.mms([(b.ap, HV[:, tk], W[0], True, False), (b.ap, HV[:, tl], W[0], False, False),
                            (b.ap, HV[:, tk], W[1], False, True)], W[2], thq[2], b.free)
            t = self.fn(VM[:, tb, :], b.ap, ACT.Identity, tok, f0, sct[0])
            b.free = [t]
            tvm.append(t)
        self.W.done(tok)
        ys_done = self.pe_now()
        tail, turned, ys, ex = {}, {}, {}, {}

        def scores(n):
            h, second = n % 8, n >= 8
            b = bk[4 + n % 2]
            if not second:
                r = slice(64 * (h % 2), 64 * (h % 2) + 64)
                t = self.mms([(b.ap[:, 0:128], QA[r, h // 2, 0:128], KA[r, h // 2, 0:128], True, True),
                              (b.ap[:, 128:384], QA[r, h // 2, 128:256], KA[r, h // 2, :], True, True)],
                             tqa, tka, b.free)
            else:
                r = slice(0, 96)
                t = self.mms([(b.ap[:, 0:128], QM[r, h, 0:128], KM[r, h, 0:128], True, True),
                              (b.ap[:, 128:384], QM[r, h, 128:256], KM[r, h, :], True, True)],
                             tqm[h], tkm, tkr, b.free)
            q = self.tmp.take()
            s = q.ap[:, 0:384]
            if not second:
                t = self.stt(s, b.ap[:, 0:384], 0.125, self.Bz[:, h, :], ALU.mult, ALU.add, t, self.bias_t, q.free)
                b.free = [t]
                t = self.tt(s, s, sc, ALU.add, t, top["sel"])
            else:
                t = self.stt(s, b.ap[:, 0:384], 96.0 ** -0.5, cm, ALU.mult, ALU.add, t, q.free)
                b.free = [t]
            st = self.stat(n)
            t1 = self.red(st[:, 0:1], s[:, 0:128], t)
            t2 = self.red(st[:, 1:2], s[:, 128:384], t)
            t3 = self.ts(st[:, 2:4], st[:, 0:2], -1.0, None, ALU.mult, None, t1, t2)
            ex[n], tb = self.exps(n, s[:, 0:128], s[:, 128:384], st, 1.0, t3)
            q.release([tb])

        def value(n):
            h, second = n % 8, n >= 8
            vv = VM if second else VA
            v = [vv[:, k, 64 * h:64 * h + 64] for k in range(2)]
            part = slice(64 * (h % 2), 64 * (h % 2) + 64)
            t = self.pv(v[0], v[1], turned[n], tvm if second else tva, part, first=h % 2 == 0)
            if h % 2:
                dst = (YB if second else YA)[h // 2]
                b = bk[7]
                th = self.fn(dst[:, 0:T], b.ap[:, 0:T], ACT.Identity, t, YB_[h // 2].free if second else ys_done)
                tl = self.tt(dst[:, T:2 * T], b.ap[:, 0:T], dst[:, 0:T].bitcast(F32), ALU.subtract, th)
                b.free = [tl]
                ys[n // 2] = [th, tl]

        def gate_unit(n):
            G, base, lst = (GA, o_ga, tga) if n < 8 else (GB, o_gb, tgb)
            u = n % 8
            b = bk[n // 2 % 4]
            t = self.unit(b.ap[:, (n % 2) * T:(n % 2) * T + T], cols(w, l, base + 128 * u),
                          b.free if n % 2 == 0 else None)
            if n % 2:
                t = self.fn(G[:, u - 1:u + 1, :].rearrange("p a t -> p (a t)"), b.ap, ACT.Tanh, t, f3, scale=0.5)
                b.free = [t]
                lst[u // 2] = self.ts(G[:, u - 1:u + 1, :], G[:, u - 1:u + 1, :], 0.5, 0.5, ALU.mult, ALU.add, t)

        def branch_a(n):
            W = self.W.take([("w_branch_a_2", l, 128 * k, 128, 128 * u, 128) for u in (n, n + 1) for k in range(4)])
            b = bk[n // 2 % 4]
            g = []
            for u in range(2):
                for k in range(4):
                    a = (4 * u + k) * 128
                    wh, wl = W[0][:, a:a + 128], W[1][:, a:a + 128]
                    o = b.ap[:, u * T:u * T + T]
                    g += [(o, wh, YA[k][:, 0:T], k == 0, False), (o, wh, YA[k][:, T:2 * T], False, False),
                          (o, wl, YA[k][:, 0:T], False, k == 3)]
            tok = self.mms(g, W[2], [ys[k] for k in range(4)], b.free)
            self.W.done(tok)
            o = GA[:, n:n + 2, :].rearrange("p a t -> p (a t)")
            tga[n // 2] = self.tt(o, b.ap, o, ALU.mult, tok, tga[n // 2])
            b.free = [tga[n // 2]]

        while "sel" not in top:
            self.background.pop(0)[1]()
        for n in range(18):
            if n < 16:
                scores(n)
                self.some_background(3)
                tail[n] = self.norm(ex[n])
            if 1 <= n < 17:
                turned[n - 1] = self.turn(tail[n - 1])
            if n < 16:
                gate_unit(n)
            if n in (11, 13, 15, 17):
                branch_a(n - 11)
            if 1 <= n < 17:
                value(n - 1)
        self.sc_free = [top["sel"]]
        self.xs_free = [self.pe_now()]
        outs = {}

        def emit_out(k):
            return self.out_k(k, 8, "w_out_2", l, self.xh(k), self.xl(k), outs[k])

        for n in range(0, 8, 2):
            W = self.W.take([("w_branch_b_2", l, 128 * k, 128, 128 * u, 128) for u in (n, n + 1) for k in range(4)])
            b = bk[4 + n // 2 % 4]
            g = []
            for u in range(2):
                for k in range(4):
                    a = (4 * u + k) * 128
                    wh, wl = W[0][:, a:a + 128], W[1][:, a:a + 128]
                    o = b.ap[:, u * T:u * T + T]
                    g += [(o, wh, YB[k][:, 0:T], k == 0, False), (o, wh, YB[k][:, T:2 * T], False, False),
                          (o, wl, YB[k][:, 0:T], False, k == 3)]
            tok = self.mms(g, W[2], [ys[k] for k in range(4, 8)], b.free)
            self.W.done(tok)
            q = self.tmp.take()
            f = lambda x: x[:, n:n + 2, :].rearrange("p a t -> p (a t)")
            t2 = self.tt(q.ap, b.ap, f(GB), ALU.mult, tok, tgb[n // 2], q.free)
            b.free = [t2]
            t = self.tt(q.ap, q.ap, f(GA), ALU.add, tga[n // 2], t2)
            for u in range(2):
                src = q.ap[:, u * T:u * T + T]
                th = self.act.do(lambda e, k=n + u, src=src: e.copy(self.xh(k), src), t, self.xs_free)
                tl = self.tt(self.xl(n + u), src, self.xh(n + u).bitcast(F32), ALU.subtract, th)
                outs[n + u] = [th, tl]
            q.release(outs[n] + outs[n + 1])
            if n >= 2:
                emit_out(n - 2)
                emit_out(n - 1)
        for o in YB_:
            o.release([self.pe_now()])
        emit_out(6)
        tok = emit_out(7)
        self.xs_free = [tok]
        fin = [tok, t]
        self.bfree = [fin, fin, fin, fin]
        self.ys_free = fin
        self.post_norm(l, 0, tok)

    def ffn(self, l):
        m, c = self.m, self.c
        outs = {}

        def emit_out(k):
            o, wt = outs[k]
            tok = self.out_k(k, 22, "w_down_2", l, o.ap[:, 0:T], o.ap[:, T:2 * T], wt)
            o.release([tok])
            return tok

        for i in range(0, 22, 2):
            acc = []
            for v in range(2):
                bank = (4 if i % 4 == 0 else 6) + v
                b = self.bank[bank]
                t = self.pair(bank, "w_up_2", l, (22 * v + i) * 128, (22 * v + i + 1) * 128)
                a = self.tmp.take()
                ta = []
                for k in range(2):
                    ch = 22 * v + i + k
                    ta.append(self.fn(a.ap[:, k * T:k * T + T], b.ap[:, k * T:k * T + T], ACT.Identity, t, a.free,
                                      scale=c(f"conv_w{l}", 88 + ch), bias=c(f"conv_b{l}", ch)))
                both = list(ta)
                for s in (1, 2):
                    for k in range(2):
                        ch = 22 * v + i + k
                        o = a.ap[:, k * T + s:k * T + T]
                        ta[k] = self.stt(o, b.ap[:, k * T:k * T + T - s], c(f"conv_w{l}", (2 - s) * 44 + ch), o,
                                         ALU.mult, ALU.add, both, ta[k])
                b.free = [ta[1]]
                acc.append((a, ta))
                self.some_background(3)
                if i >= 2:
                    emit_out(i - 2 + v)
            (g, tg), (v, tv) = acc
            t = self.fn(g.ap, g.ap, ACT.Silu, tg)
            t = self.tt(g.ap, g.ap, v.ap, ALU.mult, t, tv)
            v.release([t])
            for k in range(2):
                outs[i + k] = self.split_out(g.ap[:, k * T:k * T + T], t)
            g.release(outs[i][1] + outs[i + 1][1])
        self.xs_free = [self.pe_now()]
        emit_out(20)
        tok = emit_out(21)
        self.post_norm(l, 1, tok)

    def run(self):
        m = self.m
        self.mod_t, self.sc_free, self.ys_free, self.sm_free = [[], []], [], [], []
        s = self.s
        sp = self.sp
        tx = sp.dma(lambda e: e.dma_start(m["X"][:], self.xin), s["x"], 16)
        self.tconst = sp.dma(lambda e: e.dma_start(m["C"][:], self.cst), s["const"], 16)
        self.tpos = sp.dma(lambda e: e.dma_start(m["pos"][:], self.posr), s["pos"], 16)
        self.act.wait(tx)
        for e in (self.pe, self.dve):
            e.wait(self.tconst, tx)
        self.W = Weights(self, self.known)
        self.xt = [tx] * 8
        tcb = sp.dma(lambda e: e.dma_start(m["cb"][:], self.cbr), s["cb"], 16)
        self.tcb = tcb
        self.layer_a(0)
        self.later(self.make_bias())
        self.later(self.ada(0))
        self.layer_b()
        self.layer_c()
        self.some_background()
        self.layer_a(1)
        self.first_modulate()
        self.later(self.ada(1))
        for l in range(2):
            self.mixer(l)
            self.ffn(l)
        n = self.ndbg if self.dbg is not None else 0
        t = sp.dma(lambda e: e.dma_start(self.out, m["X"][:]), s["out"], 16 * (n + 1), self.xt)
        sp.wait(t)


def constants(inp):
    C = np.zeros((128, NCONST), np.float32)

    def put(name, a):
        o, n = COFF[name]
        a = np.asarray(a)
        C[0:a.shape[0], o:o + n] = a

    def vec(a):
        return np.asarray(a).reshape(-1, 128).T

    for j in range(2):
        put(f"a_norm{j}", vec(inp["a_norm"][j]))
        put(f"a_conv_w{j}", vec(inp["a_conv_w"][j]))
        for n in ("a_conv_b", "a_ln_g", "a_ln_b"):
            put(f"{n}{j}", vec(inp[n][j]))
    for n in ("b_norm", "b_q_norm", "b_k_norm", "c_norm", "c_conv_w"):
        put(n, vec(inp[n][0]))
    put("b_f_bias", np.asarray(inp["b_f_bias"][0]).reshape(16, 1))
    for l in range(2):
        put(f"b_ada{l}", vec(inp["b_ada_2"][l]))
        put(f"conv_w{l}", vec(inp["conv_w_2"][l]))
        put(f"conv_b{l}", vec(inp["conv_b_2"][l]))
        for n in ("ln1_g", "ln1_b", "ln2_g", "ln2_b"):
            put(f"{n}{l}", vec(inp[n + "_2"][l]))
        put(f"q_norm{l}", vec(inp["q_norm_g_2"][l]))
        put(f"kv_norm{l}", vec(inp["kv_norm_g_2"][l]))
    put("rel_bias", np.broadcast_to(np.asarray(inp["rel_bias_2"]).reshape(1, 256), (128, 256)))
    put("ident", np.eye(128, dtype=np.float32))
    tri = np.where(np.arange(128)[None, :] <= np.arange(128)[:, None], 0.0, NEG).astype(np.float32)
    put("cmask", np.concatenate([tri, np.zeros((128, 128), np.float32), tri], axis=1))
    hot = np.zeros((128, 31), np.float32)
    hot[:, 15] = 1.0
    put("onehot", hot)
    put("ones", np.ones((128, 128), np.float32))
    freq = np.float32(10000.0) ** (-np.arange(16, dtype=np.float32) * np.float32(2.0 / 32))
    col = np.zeros((128, 1), np.float32)
    col[64:80, 0] = col[80:96, 0] = freq
    put("freq", col)
    mul = np.zeros((128, 2), np.float32)
    mul[64:80, 0], mul[80:96, 0] = -1.0, 1.0
    put("ropemul", mul)
    return C


def stream(pieces, inp):
    W = np.empty((128, sum(wd for _, wd in pieces)), np.float32)
    at = 0
    for blocks, _ in pieces:
        for name, layer, r0, nr, c0, n, *turned in blocks:
            W[:, at:at + n] = inp[name][layer].T[r0:r0 + nr, c0:c0 + n] if turned else \
                inp[name][layer, r0:r0 + nr, c0:c0 + n]
            at += n
    return W


def lay(nc, arrays, dbg=None):
    pos = np.asarray(arrays["positions_2"], np.int32).reshape(T)
    posr = np.empty((128, T + 2), np.int32)
    posr[:, 0:T] = pos[None, :]
    posr[:, T:T + 2] = pos.reshape(2, 128).T
    x = np.ascontiguousarray(np.asarray(arrays["x"])[0].T.reshape(8, 128, T).transpose(1, 0, 2))
    cst = constants(arrays)
    cb = np.ascontiguousarray(np.broadcast_to(np.asarray(arrays["c_2"], np.float32).reshape(1, D), (128, D)))
    ins = {"in_cst": cst, "in_pos": posr, "in_cb": cb, "in_x": x}
    aps = {k: nc.dram_tensor(k, v.shape, mybir.dt.from_np(v.dtype), kind="ExternalInput").ap() for k, v in ins.items()}
    out = nc.dram_tensor("out_x", (128, 8, T), F32, kind="ExternalOutput").ap()

    def w_stream_of(width):
        return nc.dram_tensor("in_w", (128, width), F32, kind="ExternalInput").ap()

    pieces = build(nc, w_stream_of, aps["in_cst"], aps["in_pos"], aps["in_cb"], aps["in_x"], out, dbg)
    ins["in_w"] = stream(pieces, arrays)
    return ins


def kernel(**inputs):
    import concourse.bacc as _bacc
    from concourse.bass_utils import run_bass_kernel_spmd as _run

    nc = _bacc.Bacc("TRN2", target_bir_lowering=False, num_devices=1)
    arrays = {k: np.asarray(v) for k, v in inputs.items()}
    ins = lay(nc, arrays)
    r = _run(nc, [ins], core_ids=[0])
    y = r.results[0]["out_x"]
    return np.ascontiguousarray(y.transpose(1, 0, 2).reshape(D, T).T).reshape(1, T, D)
```
